# Optimizing a Trainium2 kernel written in Bass

```python
import math
import jax, jax.numpy as jnp
from jax import lax
import numpy as np

D_MODEL = 1024
BATCH = 1
SEQ = 512
DEPTH = 1

ATT_HEADS = 8
ATT_KV_HEADS = 2
ATT_HEAD_DIM = 64
ROT_DIM = ATT_HEAD_DIM // 4
ROPE_THETA = 500000.0
WINDOW = 128
ATT_BLOCK = 128
HG_HEADS = 4
HG_DIM = 128
HG_CHUNK = 64
ATT_WIDTH = ATT_HEADS * ATT_HEAD_DIM
KV_WIDTH = ATT_KV_HEADS * ATT_HEAD_DIM
HG_WIDTH = HG_HEADS * HG_DIM
MIX_WIDTH = ATT_WIDTH + HG_WIDTH
IN_SIZES = (ATT_WIDTH, KV_WIDTH, KV_WIDTH, HG_WIDTH, HG_WIDTH, HG_WIDTH, HG_WIDTH, HG_WIDTH)
IN_WIDTH = ATT_WIDTH + 2 * KV_WIDTH + 5 * HG_WIDTH
D_FF = 2816
FFN_RES_WEIGHT = 0.5
EPS = 1e-6
NEG_INF = -1e30

kernel_name = "hymba_swa_hgrn2_macaron_encoder"

def rmsnorm(x, w):
    xf = x.astype(jnp.float32)
    y = xf * lax.rsqrt(jnp.mean(xf * xf, axis=-1, keepdims=True) + EPS)
    return (y * w.astype(jnp.float32)).astype(x.dtype)

def swiglu(x, w_gate, w_up, w_down):
    return (jax.nn.silu(x @ w_gate) * (x @ w_up)) @ w_down

def partial_rope(t, pos):
    half = ROT_DIM // 2
    inv_freq = jnp.exp(-math.log(ROPE_THETA) * jnp.arange(half, dtype=jnp.float32) * 2.0 / ROT_DIM)
    ang = pos[:, None] * inv_freq[None, :]
    cos = jnp.cos(ang)[None, :, None, :]
    sin = jnp.sin(ang)[None, :, None, :]
    tf = t.astype(jnp.float32)
    t1, t2, rest = tf[..., :half], tf[..., half:ROT_DIM], tf[..., ROT_DIM:]
    return jnp.concatenate([t1 * cos - t2 * sin, t2 * cos + t1 * sin, rest], axis=-1).astype(t.dtype)

def windowed_gqa_sink(q, k, v, sink):
    B, S = q.shape[0], q.shape[1]
    nb = S // ATT_BLOCK
    G = ATT_HEADS // ATT_KV_HEADS
    qb = q.reshape(B, nb, ATT_BLOCK, ATT_KV_HEADS, G, ATT_HEAD_DIM)
    pad = ((0, 0), (ATT_BLOCK, ATT_BLOCK), (0, 0), (0, 0))
    kp = jnp.pad(k, pad).reshape(B, nb + 2, ATT_BLOCK, ATT_KV_HEADS, ATT_HEAD_DIM)
    vp = jnp.pad(v, pad).reshape(B, nb + 2, ATT_BLOCK, ATT_KV_HEADS, ATT_HEAD_DIM)

    def band(t):
        return jnp.concatenate([t[:, :-2], t[:, 1:-1], t[:, 2:]], axis=2)

    kb, vb = band(kp), band(vp)
    blk = jnp.arange(nb)
    q_pos = blk[:, None, None] * ATT_BLOCK + jnp.arange(ATT_BLOCK)[None, :, None]
    k_pos = blk[:, None, None] * ATT_BLOCK - ATT_BLOCK + jnp.arange(3 * ATT_BLOCK)[None, None, :]
    valid = (k_pos >= 0) & (k_pos < S) & (jnp.abs(k_pos - q_pos) <= WINDOW)
    sink_f = sink.astype(jnp.float32).reshape(ATT_KV_HEADS, G)[None, :, :, None, None]
    scale = ATT_HEAD_DIM ** -0.5

    def one_block(args):
        qn, kn, vn, mn = args
        s = jnp.einsum('bqhgd,bkhd->bhgqk', qn, kn).astype(jnp.float32) * scale
        s = jnp.where(mn, s, NEG_INF)
        m = jnp.maximum(jnp.max(s, axis=-1, keepdims=True), sink_f)
        p = jnp.exp(s - m)
        p = p / (jnp.sum(p, axis=-1, keepdims=True) + jnp.exp(sink_f - m))
        return jnp.einsum('bhgqk,bkhd->bqhgd', p.astype(vn.dtype), vn)

    o = lax.map(one_block, (jnp.moveaxis(qb, 1, 0), jnp.moveaxis(kb, 1, 0), jnp.moveaxis(vb, 1, 0), valid))
    return jnp.moveaxis(o, 0, 1).reshape(B, S, ATT_WIDTH)

def gla_chunk_scan(q, k, v, log_f):
    B, S, H, DK = q.shape
    DV = v.shape[-1]
    n = S // HG_CHUNK

    def chunks(t):
        return t.reshape(B, n, HG_CHUNK, H, t.shape[-1]).transpose(1, 0, 3, 2, 4)

    mask = jnp.tril(jnp.ones((HG_CHUNK, HG_CHUNK), dtype=bool))[:, :, None]

    def step(state, xs):
        qc, kc, vc, gc = xs
        b = jnp.cumsum(gc, axis=2)
        decay = jnp.exp(jnp.where(mask, b[:, :, :, None, :] - b[:, :, None, :, :], NEG_INF))
        scores = jnp.einsum('bhtsk,bhsk->bhts', qc[:, :, :, None, :] * decay, kc)
        o = (jnp.einsum('bhts,bhsv->bhtv', scores, vc)
             + jnp.einsum('bhtk,bhkv->bhtv', qc * jnp.exp(b), state))
        b_last = b[:, :, -1:, :]
        state = (state * jnp.exp(b_last)[:, :, 0, :, None]
                 + jnp.einsum('bhsk,bhsv->bhkv', kc * jnp.exp(b_last - b), vc))
        return state, o

    state0 = jnp.zeros((B, H, DK, DV), jnp.float32)
    _, o = lax.scan(step, state0, (chunks(q), chunks(k), chunks(v), chunks(log_f)))
    return o.transpose(1, 0, 3, 2, 4).reshape(B, S, H, DV)

def hgrn2_direction(q, v, f_logit, lb):
    f = lb + (1.0 - lb) * jax.nn.sigmoid(f_logit)
    return gla_chunk_scan(q, 1.0 - f, v, jnp.log(f))

def layer_lower_bound(lb_raw, layer):
    return jnp.cumsum(jax.nn.softmax(lb_raw.astype(jnp.float32), axis=0), axis=0)[layer]

def hybrid_mixer(u, w_in, attn_sink, attn_out_norm, lb_fwd, lb_bwd, hg_out_norm, w_out, layer):
    B, S, _ = u.shape
    proj = u @ w_in
    cuts, acc = [], 0
    for size in IN_SIZES[:-1]:
        acc += size
        cuts.append(acc)
    q, k, v, hq, hf_fwd, hf_bwd, hi, hg = jnp.split(proj, cuts, axis=-1)

    pos = jnp.arange(S, dtype=jnp.float32)
    q = partial_rope(q.reshape(B, S, ATT_HEADS, ATT_HEAD_DIM), pos)
    k = partial_rope(k.reshape(B, S, ATT_KV_HEADS, ATT_HEAD_DIM), pos)
    v = v.reshape(B, S, ATT_KV_HEADS, ATT_HEAD_DIM)
    att = rmsnorm(windowed_gqa_sink(q, k, v, attn_sink), attn_out_norm)

    heads = lambda t: t.reshape(B, S, HG_HEADS, HG_DIM).astype(jnp.float32)
    qh = jax.nn.sigmoid(heads(hq))
    vh = jax.nn.silu(heads(hi))
    lbf = layer_lower_bound(lb_fwd, layer).reshape(HG_HEADS, HG_DIM)
    lbb = layer_lower_bound(lb_bwd, layer).reshape(HG_HEADS, HG_DIM)
    o_fwd = hgrn2_direction(qh, vh, heads(hf_fwd), lbf)
    flip = lambda t: jnp.flip(t, axis=1)
    o_bwd = flip(hgrn2_direction(flip(qh), flip(vh), flip(heads(hf_bwd)), lbb))
    o = rmsnorm(o_fwd + o_bwd, hg_out_norm) * jax.nn.silu(heads(hg))
    hgo = o.reshape(B, S, HG_WIDTH).astype(u.dtype)

    return jnp.concatenate([att, hgo], axis=-1) @ w_out

def setup_inputs(seed: int = 0) -> dict:
    key = jax.random.key(seed)
    ks = jax.random.split(key, 24)
    f32 = jnp.float32

    def w(k, shape, fan_in):
        return jax.random.normal(k, shape, f32) * (fan_in ** -0.5)

    def gain(k, shape):
        return 1.0 + 0.02 * jax.random.normal(k, shape, f32)

    return {
        "x": jax.random.normal(ks[0], (BATCH, SEQ, D_MODEL), f32),
        "ffn1_pre_norm": gain(ks[1], (DEPTH, D_MODEL)),
        "ffn1_post_norm": gain(ks[2], (DEPTH, D_MODEL)),
        "ffn1_w_gate": w(ks[3], (DEPTH, D_MODEL, D_FF), D_MODEL),
        "ffn1_w_up": w(ks[4], (DEPTH, D_MODEL, D_FF), D_MODEL),
        "ffn1_w_down": w(ks[5], (DEPTH, D_FF, D_MODEL), D_FF),
        "mix_pre_norm": gain(ks[6], (DEPTH, D_MODEL)),
        "mix_post_norm": gain(ks[7], (DEPTH, D_MODEL)),
        "w_in": w(ks[8], (DEPTH, D_MODEL, IN_WIDTH), D_MODEL),
        "attn_sink": 0.5 * jax.random.normal(ks[9], (DEPTH, ATT_HEADS), f32),
        "attn_out_norm": gain(ks[10], (DEPTH, ATT_WIDTH)),
        "hgrn_lb_fwd": 0.1 * jax.random.normal(ks[11], (DEPTH + 1, HG_WIDTH), f32),
        "hgrn_lb_bwd": 0.1 * jax.random.normal(ks[12], (DEPTH + 1, HG_WIDTH), f32),
        "hgrn_out_norm": gain(ks[13], (DEPTH, HG_DIM)),
        "w_out": w(ks[14], (DEPTH, MIX_WIDTH, D_MODEL), MIX_WIDTH),
        "ffn2_pre_norm": gain(ks[15], (DEPTH, D_MODEL)),
        "ffn2_post_norm": gain(ks[16], (DEPTH, D_MODEL)),
        "ffn2_w_gate": w(ks[17], (DEPTH, D_MODEL, D_FF), D_MODEL),
        "ffn2_w_up": w(ks[18], (DEPTH, D_MODEL, D_FF), D_MODEL),
        "ffn2_w_down": w(ks[19], (DEPTH, D_FF, D_MODEL), D_FF),
    }

def reference(x, ffn1_pre_norm, ffn1_post_norm, ffn1_w_gate, ffn1_w_up, ffn1_w_down,
              mix_pre_norm, mix_post_norm, w_in, attn_sink, attn_out_norm,
              hgrn_lb_fwd, hgrn_lb_bwd, hgrn_out_norm, w_out,
              ffn2_pre_norm, ffn2_post_norm, ffn2_w_gate, ffn2_w_up, ffn2_w_down):
    for l in range(DEPTH):
        h = swiglu(rmsnorm(x, ffn1_pre_norm[l]), ffn1_w_gate[l], ffn1_w_up[l], ffn1_w_down[l])
        x = x + FFN_RES_WEIGHT * rmsnorm(h, ffn1_post_norm[l])
        h = hybrid_mixer(rmsnorm(x, mix_pre_norm[l]), w_in[l], attn_sink[l], attn_out_norm[l],
                         hgrn_lb_fwd, hgrn_lb_bwd, hgrn_out_norm[l], w_out[l], l)
        x = x + rmsnorm(h, mix_post_norm[l])
        h = swiglu(rmsnorm(x, ffn2_pre_norm[l]), ffn2_w_gate[l], ffn2_w_up[l], ffn2_w_down[l])
        x = x + FFN_RES_WEIGHT * rmsnorm(h, ffn2_post_norm[l])
    return x


_drawn_inputs = setup_inputs


def setup_inputs(seed=0):
    import zlib

    import numpy as np

    out = dict(_drawn_inputs(seed))
    spreads = {}
    factors = {'ffn1_pre_norm': 3.014,
     'ffn1_post_norm': 4.543,
     'mix_post_norm': 11.357,
     'attn_sink': 8.0,
     'attn_out_norm': 55.595,
     'hgrn_lb_fwd': 153.344,
     'hgrn_lb_bwd': 32.487,
     'hgrn_out_norm': 95.633,
     'ffn2_pre_norm': 19.771,
     'ffn2_post_norm': 121.066}
    for name, (base, spread) in spreads.items():
        noise = np.random.default_rng([zlib.crc32(name.encode()), seed]).standard_normal(out[name].shape)
        drawn = base * np.exp(spread * noise) if base else spread * noise
        out[name] = __import__('jax').numpy.asarray(drawn.astype(out[name].dtype))
    for name, factor in factors.items():
        out[name] = (out[name] * factor).astype(out[name].dtype)
    return out
```

```python
import numpy as np
import concourse.bass as bass
from concourse import mybir
from contextlib import ExitStack

P = 128
TOK = 512
D = 1024
F = 2816
KD = D // P
KF = F // P
TT = TOK // P
HQ, HKV, DH = 8, 2, 64
G = HQ // HKV
NH = 4
ROT = 16
THETA = 500000.0
WINDOW = 128
EPS = 1e-6
SCALE = DH ** -0.5
NSLOT = 4
KSPLIT = ((0, 8), (8, 7), (15, 7))
BIG = 8e30

SLOT = KD * P

C_Q, C_K, C_V = 0, 512, 640
C_HQ, C_HFF, C_HFB, C_HI, C_HG = 768, 1280, 1792, 2304, 2816

N_UP = 2 * KF
N_DOWN = len(KSPLIT) * KD
FFN1 = 0
MIX = N_UP + N_DOWN
MIX_UNITS = 26
TAKEN_QKV = 3 * NH + TT
OUT = MIX + MIX_UNITS
FFN2 = OUT + KD


def mixer_units():
    units = []
    for h in range(NH):
        units += [("f", c + h * P) for c in (C_HQ, C_HFF, C_HFB)]
        if h == 0:
            units += [("w", C_HI, 2 * k) for k in range(4)]
    units += [("f", C_K), ("f", C_V)]
    units += [("q", j) for j in range(G)]
    units += [("w", C_HG, 2 * k) for k in range(4)]
    return units


def host_tables():
    pos = np.arange(TOK, dtype=np.float32)
    half = ROT // 2
    inv = np.exp(np.float32(-np.log(THETA)) * np.arange(half, dtype=np.float32) * np.float32(2.0 / ROT)).astype(np.float32)
    ang = (pos[:, None] * inv[None, :]).astype(np.float32).astype(np.float64)
    cos = np.ones((P, TOK), np.float32)
    sin = np.zeros((P, TOK), np.float32)
    swap = np.zeros((P, P), np.float32)
    for s in range(2):
        for d in range(half):
            a, b = s * DH + d, s * DH + half + d
            cos[a] = cos[b] = np.cos(ang[:, d])
            sin[a] = sin[b] = np.sin(ang[:, d])
            swap[b, a] = -1.0
            swap[a, b] = 1.0
    ident = np.eye(P, dtype=np.float32)
    q = np.arange(P)[:, None]
    k = np.arange(3 * P)[None, :] - P
    band = np.where(np.abs(k - q) <= WINDOW, 0.0, -BIG).astype(np.float32)
    levels = []
    s = np.arange(P)
    for lv in range(7):
        h = 1 << lv
        m = np.zeros((P, 2, TT, P // (2 * h), h), np.float32)
        for side in range(2):
            for b in range(P // (2 * h)):
                hit = (s // (2 * h) == b) & ((s // h) % 2 != side)
                m[:, side, :, b, :] = hit[:, None, None]
        levels.append(m.reshape(P, TOK))
    return {
        "t_square": np.ascontiguousarray(np.concatenate([ident, swap, band], 1)),
        "t_rope": np.ascontiguousarray(np.concatenate([cos, sin], 1)),
        "t_mask": np.ascontiguousarray(np.stack(levels, 1)),
    }


def encoder_layer(nc, io, out):
    fp32, f32r, u8 = mybir.dt.float32, mybir.dt.float32r, mybir.dt.uint8
    ALU, ACT, AX = mybir.AluOpType, mybir.ActivationFunctionType, mybir.AxisListType
    ctx = ExitStack()
    with ctx:
        def sb(name, shape, dt=fp32, to=ctx):
            return to.enter_context(nc.sbuf_tensor(name, shape, dt))

        def sem(name):
            return ctx.enter_context(nc.semaphore(name))

        xT = sb("xT", [P, KD, TOK])
        raw = sb("raw", [P, NSLOT, SLOT])
        WH, WL = sb("WH", [P, NSLOT, SLOT], f32r), sb("WL", [P, NSLOT, SLOT], f32r)
        NV = 6 * KD + 4 * NH + 4
        vec_rows = sb("vec_rows", [NV, P])
        vecs = sb("vecs", [P, NV])
        gains = vecs[:, 0:6 * KD].rearrange("p (v k) -> p v k", k=KD)
        lbr = vecs[:, 6 * KD:6 * KD + 4 * NH].rearrange("p (d r h) -> p d r h", d=2, r=2)
        attgain = vecs[:, 6 * KD + 4 * NH:NV]
        sink = sb("sink", [P, HQ])
        HGN = sb("HGN", [P, P])
        small = sb("small", [P, 256])
        ident = sb("ident", [P, P])
        ones, eps = sb("ones", [P, 1]), sb("eps", [P, 1])
        rt_root, rt = sb("rt_root", [P, 6, TT]), sb("rt", [P, 6, TT])
        RSB = sb("RSB", [P, TOK])
        TMP = sb("TMP", [P, 2, TOK])
        SQ = sb("SQ", [P, 2, TOK])
        SQX = sb("SQX", [P, 2, TOK])
        SS, SSX = sb("SS", [P, TOK]), sb("SSX", [P, TOK])
        XH = sb("XH", [P, KD, TOK], f32r)
        with nc.sbuf_tensor("YB", [P, KD, TOK], fp32) as YB:
            pass
        XL = sb("XL", [P, KD, TOK], f32r)
        ps = [ctx.enter_context(nc.psum_tensor(f"ps{b}", [P, 512], fp32)) for b in range(8)]
        STAT, BC = ps[6], ps[7]
        turn = (ps[4], ps[5], ps[7])

        def place(*wanted):
            with ExitStack() as region:
                return [region.enter_context(nc.sbuf_tensor(n, s, d)) for n, s, d in wanted]

        hid = [place((f"hh{f}", [P, KF, TOK], f32r), (f"hl{f}", [P, KF, TOK], f32r)) for f in (1, 2)]
        xin, = place(("xin", [P, TT, D], fp32))
        xout, = place(("xout", [P, TT, D], fp32))
        common = [("V", [P, TT, TOK], fp32), ("OS", [P, TT, TOK], fp32), ("rope", [P, 2, TOK], fp32),
                  ("qT", [P, G, TOK], fp32), ("kT", [P, TOK], fp32), ("VA", [P, TT, P], fp32),
                  ("swap", [P, P], fp32), ("band", [P, 3 * P], fp32)]
        V, OS, rope, qT, kT, VA, swap, band, W, GT, Fg, Qh, KS, SD, SX, masks = place(
            *common, ("W", [P, 2, 4, TOK], fp32), ("GT", [P, 2, TOK], fp32), ("Fg", [P, 2, 2, TOK], fp32),
            ("Qh", [P, 2, TOK], fp32), ("KS", [P, 2, TOK], fp32), ("SD", [P, TOK], fp32),
            ("SX", [P, 3, TOK], fp32), ("masks", [P, 7, TOK], u8))
        *_, ATT, HGATE, S, PT = place(
            *[(n + "_", s, d) for n, s, d in common], ("ATT", [P, TT, TOK], fp32), ("HGATE", [P, TT, TOK], fp32),
            ("S", [P, HQ, 3 * P], fp32), ("PT", [P, 2, 3 * P], fp32))
        mask_in, = place(("mask_in", [P, 7, TOK], fp32))
        YM, = place(("YM", [P, KD, TOK], fp32))
        lbm, lbs = small[:, 0:8], small[:, 8:16]
        lb, lb1 = small[:, 16:24], small[:, 24:32]
        m8, nm8, l8, e8, r8 = (small[:, 48 + 8 * n:56 + 8 * n] for n in range(5))
        oss, oroot, orr = (small[:, 112 + 16 * n:128 + 16 * n] for n in range(3))
        ass, aroot, arr = (small[:, 160 + 4 * n:164 + 4 * n] for n in range(3))

        raw_full = [sem(f"raw_full{s}") for s in range(NSLOT)]
        hi_done, lo_done = sem("hi_done"), sem("lo_done")
        unit_used = sem("unit_used")
        second_full = [sem(f"second_full{j}") for j in range(G)]
        const_in, mix_in, x_in = sem("const_in"), sem("mix_in"), [sem(f"x_in{c}") for c in range(TT)]
        CONST_IN, MIX_IN = 12 * 16, 4 * 16
        set_up = sem("set_up")
        x_turned = sem("x_turned")
        x_ready, xh_ready, xl_ready = sem("x_ready"), sem("xh_ready"), sem("xl_ready")
        x_squared, x_summed = sem("x_squared"), sem("x_summed")
        y_copied, y_squared, y_summed = sem("y_copied"), sem("y_squared"), sem("y_summed")
        stat_ready, root_ready, rt_ready, bc_ready, rsb_ready = (
            sem(n) for n in ("stat_ready", "root_ready", "rt_ready", "bc_ready", "rsb_ready"))
        gate_scaled, up_scaled, gate_sig, h_ready = (sem(n) for n in ("gate_scaled", "up_scaled", "gate_sig", "h_ready"))
        vchain, achain, pchain = sem("vchain"), sem("achain"), sem("pchain")
        proj_taken, proj_sig = sem("proj_taken"), sem("proj_sig")
        f_ready, tree_ready = sem("f_ready"), sem("tree_ready")
        scores_ready, scores_masked, scores_copied = sem("scores_ready"), sem("scores_masked"), sem("scores_copied")
        pv_done, o_copied = sem("pv_done"), sem("o_copied")
        rot_ready, rope_done, va_turned, va_ready = (sem(n) for n in ("rot_ready", "rope_done", "va_turned", "va_ready"))
        s_ready, s_max, s_exp, s_soft = (sem(n) for n in ("s_ready", "s_max", "s_exp", "s_soft"))
        pt_ready, pt_even, pt_odd, att_pv_done, att_scaled = (
            sem(n) for n in ("pt_ready", "pt_even", "pt_odd", "att_pv_done", "att_scaled"))
        nm_ready, att_sq, osq, oroot_ready, mixT, mix_turned, mixh, mixl = (
            sem(n) for n in ("nm_ready", "att_sq", "osq", "oroot_ready", "mixT", "mix_turned", "mixh", "mixl"))
        wide_sig, vecs_turned = sem("wide_sig"), sem("vecs_turned")
        out_turned, out_copied, out_copied_v, stored = (sem(n) for n in ("out_turned", "out_copied", "out_copied_v", "stored"))
        lb_max, lb_exp = sem("lb_max"), sem("lb_exp")

        w_of = {s: (io[f"ffn{s}_w_gate"][0].rearrange("(k p) f -> p k f", p=P),
                    io[f"ffn{s}_w_up"][0].rearrange("(k p) f -> p k f", p=P),
                    io[f"ffn{s}_w_down"][0].rearrange("(k p) f -> p k f", p=P)) for s in (1, 2)}
        w_in = io["w_in"][0].rearrange("(k p) f -> p k f", p=P)
        w_out = io["w_out"][0].rearrange("(k p) f -> p k f", p=P)
        MIXU = mixer_units()
        block = ctx.enter_context(nc.Block())

        def turns(n, quarter=0):
            return quarter + (n // NSLOT + 1)

        @block.sync
        def _(sp):
            def load(n, quarter, src):
                if n >= NSLOT:
                    sp.wait_ge(lo_done, quarter * NSLOT + (n - NSLOT + 1))
                nk = src.shape[1]
                dst = raw[:, n % NSLOT, 0:nk * src.shape[2]].rearrange("p (k f) -> p k f", k=nk)
                sp.dma_start(dst, src).then_inc(raw_full[n % NSLOT], 16)

            def load_pair(n, j):
                sp.wait_ge(lo_done, n - NSLOT + 1)
                dst = raw[:, n % NSLOT, :].rearrange("p (k s d) -> p s k d", k=KD, s=HKV)
                for s, full in enumerate((raw_full[n % NSLOT], second_full[j])):
                    c = C_Q + (s * G + j) * DH
                    sp.dma_start(dst[:, s], w_in[:, :, c:c + DH]).then_inc(full, 16)

            def load_ffn(s, first):
                gate, up, down = w_of[s]
                for b in range(NSLOT):
                    load(first + b, 0, (gate, up)[b % 2][:, :, (b // 2) * P:(b // 2 + 1) * P])
                with sp.Fori(0, KF // 2 - 1) as i:
                    for b in range(NSLOT):
                        load(first + NSLOT + b, i, (gate, up)[b % 2][:, :, bass.ds(i * (2 * P) + (2 + b // 2) * P, P)])
                for m in range(KD):
                    for u, (k0, nk) in enumerate(KSPLIT):
                        load(first + N_UP + len(KSPLIT) * m + u, 0, down[:, k0:k0 + nk, m * P:(m + 1) * P])

            row = 0
            for name in ("ffn1_pre_norm", "ffn1_post_norm", "mix_pre_norm", "mix_post_norm", "ffn2_pre_norm", "ffn2_post_norm"):
                sp.dma_start(vec_rows[row:row + KD, :], io[name][0].rearrange("(k p) -> k p", p=P)).then_inc(const_in, 16)
                row += KD
            for name in ("hgrn_lb_fwd", "hgrn_lb_bwd"):
                sp.dma_start(vec_rows[row:row + 2 * NH, :], io[name].rearrange("r (h p) -> (r h) p", p=P)).then_inc(const_in, 16)
                row += 2 * NH
            sp.dma_start(vec_rows[row:row + 4, :], io["attn_out_norm"][0].rearrange("(k p) -> k p", p=P)).then_inc(const_in, 16)
            sp.dma_start(ident[:, :], io["t_square"][:, 0:P]).then_inc(const_in, 16)
            sp.dma_start(sink[:, :], io["attn_sink"][0].partition_broadcast(P)).then_inc(const_in, 16)
            sp.dma_start(HGN[:, :], io["hgrn_out_norm"][0].partition_broadcast(P)).then_inc(const_in, 16)
            for c in range(TT):
                sp.dma_start(xin[:, c, :], io["x"][0, c * P:(c + 1) * P, :]).then_inc(x_in[c], 16)
            load_ffn(1, FFN1)
            for u, unit in enumerate(MIXU):
                if u == 0:
                    sp.wait_ge(unit_used, MIX)
                    sp.dma_start(mask_in[:, :, :], io["t_mask"]).then_inc(mix_in, 16)
                    sp.dma_start(rope[:, :, :], io["t_rope"].rearrange("p (a t) -> p a t", a=2)).then_inc(mix_in, 16)
                    sp.dma_start(swap[:, :], io["t_square"][:, P:2 * P]).then_inc(mix_in, 16)
                    sp.dma_start(band[:, :], io["t_square"][:, 2 * P:5 * P]).then_inc(mix_in, 16)
                if unit[0] == "f":
                    load(MIX + u, 0, w_in[:, :, unit[1]:unit[1] + P])
                elif unit[0] == "w":
                    load(MIX + u, 0, w_in[:, unit[2]:unit[2] + 2, unit[1]:unit[1] + 4 * P])
                else:
                    load_pair(MIX + u, unit[1])
            for m in range(KD):
                load(OUT + m, 0, w_out[:, :, m * P:(m + 1) * P])
            load_ffn(2, FFN2)
            sp.wait_ge(out_copied, 4)
            sp.wait_ge(out_copied_v, 4)
            sp.dma_start(out[0].rearrange("(c p) d -> p c d", p=P), xout[:, :, :]).then_inc(stored, 16)
            sp.wait_ge(stored, 16)

        @block.gpsimd
        def _(pool):
            def lo(n, quarter, size):
                pool.wait_ge(hi_done, quarter * NSLOT + (n + 1))
                s = n % NSLOT
                pool.tensor_tensor(WL[:, s, 0:size], raw[:, s, 0:size], WH[:, s, 0:size].bitcast(fp32),
                                   ALU.subtract).then_inc(lo_done, 1)

            def sum_x(e):
                if e:
                    pool.wait_ge(stat_ready, 2 * e)
                pool.memset(SSX[:, :], 0.0).then_inc(pchain, 1)
                pool.wait_ge(pchain, e + 1)
                for k in range(KD):
                    pool.wait_ge(x_squared, KD * e + k + 1)
                    if k:
                        pool.wait_ge(x_summed, KD * e + k)
                    pool.tensor_tensor(SSX[:, :], SSX[:, :], SQX[:, k % 2, :], ALU.add).then_inc(x_summed, 1)

            def lo_ffn(first, e):
                for b in range(NSLOT):
                    lo(first + b, 0, SLOT)
                sum_x(e)
                with pool.Fori(0, KF // 2 - 1) as i:
                    for b in range(NSLOT):
                        lo(first + NSLOT + b, i, SLOT)
                with pool.Fori(0, 2) as i:
                    for u in range(4 * len(KSPLIT)):
                        lo(first + N_UP + u, i * 3, KSPLIT[u % 3][1] * P)

            lo_ffn(FFN1, 0)
            for u in range(4):
                lo(MIX + u, 0, SLOT)
            sum_x(1)
            for u in range(4, MIX_UNITS + KD):
                lo(MIX + u, 0, SLOT)
            lo_ffn(FFN2, 2)

        @block.scalar
        def _(act):
            def hi(n, quarter=0, size=SLOT):
                act.wait_ge(raw_full[n % NSLOT], turns(n, quarter) * 16)
                if MIX <= n < OUT and MIXU[n - MIX][0] == "q":
                    act.wait_ge(second_full[MIXU[n - MIX][1]], 16)
                if n >= NSLOT:
                    act.wait_ge(unit_used, quarter * NSLOT + (n - NSLOT + 1))
                s = n % NSLOT
                nc.scalar.activation(WH[:, s, 0:size], raw[:, s, 0:size], ACT.Copy).then_inc(hi_done, 1)

            def unit_size(n):
                for f in (FFN1, FFN2):
                    if f + N_UP <= n < f + N_UP + N_DOWN:
                        return KSPLIT[(n - f - N_UP) % 3][1] * P
                return SLOT

            done = [0]

            def ahead(n):
                while done[0] <= min(n, FFN2 + N_UP + N_DOWN - 1):
                    hi(done[0], 0, unit_size(done[0]))
                    done[0] += 1

            def root(s):
                act.wait_ge(stat_ready, s + 1)
                nc.scalar.activation(rt_root[:, s, :], STAT[:, 0:TT], ACT.Sqrt, bias=eps[:, :], scale=1.0 / D).then_inc(root_ready, 1)

            def split_high(e, k):
                act.wait_ge(x_ready, KD * e + k + 1)
                if e < 3:
                    if not k and e:
                        act.wait_ge(unit_used, (FFN1 + N_UP + N_DOWN, OUT + KD)[e - 1])
                    nc.scalar.activation(XH[:, k, :], xT[:, k, :], ACT.Copy, scale=gains[:, 2 * e, k:k + 1]).then_inc(xh_ready, 1)
                    if k >= 2:
                        act.wait_ge(x_summed, KD * e + k - 1)
                    nc.scalar.activation(SQX[:, k % 2, :], xT[:, k, :], ACT.Square).then_inc(x_squared, 1)

            def square_y(m, count, buf):
                act.wait_ge(y_copied, count + m + 3)
                if m >= 2 or count:
                    act.wait_ge(y_summed, count + m - 1)
                nc.scalar.activation(SQ[:, m % 2, :], buf[:, m, :], ACT.Square).then_inc(y_squared, 1)

            def ffn(f, first):
                for k in range(KD):
                    split_high(2 * f, k)
                root(4 * f)

                def sig(j, a):
                    act.wait_ge(gate_scaled, j)
                    nc.scalar.activation(SQX[:, a, :], TMP[:, a, :], ACT.Sigmoid).then_inc(gate_sig, 1)

                with act.Fori(0, KF // 2 - 1) as i:
                    for a in range(2):
                        for b in range(2):
                            hi(first + NSLOT + 2 * a + b, i)
                        sig(i * 2 + (KF * f + a + 1), a)
                done[0] = first + N_UP
                for a in range(2):
                    ahead(first + N_UP + 2 * a + 1)
                    sig(KF * f + KF - 2 + a + 1, a)
                for m in range(KD):
                    ahead(first + N_UP + 3 * m + 6)
                    square_y(m, 16 * f, YB)

            ahead(3)
            act.wait_ge(set_up, 1)
            ffn(0, FFN1)
            root(1)
            act.wait_ge(lb_max, 1)
            nc.scalar.activation(lbr, lbr, ACT.Exp).then_inc(lb_exp, 1)
            for k in range(KD):
                split_high(1, k)
            root(2)

            nsig = [0]

            def psig(dst, taken):
                act.wait_ge(proj_taken, taken)
                nc.scalar.activation(dst, TMP[:, nsig[0] % 2, :], ACT.Sigmoid).then_inc(proj_sig, 1)
                nsig[0] += 1

            def wide_sigmoid(last_unit, taken):
                ahead(last_unit + 3)
                act.wait_ge(unit_used, last_unit + 1)
                for c in range(TT):
                    if c >= 2:
                        act.wait_ge(proj_taken, taken + c - 1)
                    nc.scalar.activation(SQX[:, c % 2, :], ps[c][:, :], ACT.Sigmoid, scale=rt[:, 2, c:c + 1]).then_inc(wide_sig, 1)

            taken, unit = 0, MIX
            for h in range(NH):
                for t in range(3):
                    ahead(unit + 3)
                    psig(Qh[:, h % 2, :] if t == 0 else Fg[:, h % 2, t - 1, :], taken + 1)
                    taken += 1
                    unit += 1
                if h == 0:
                    wide_sigmoid(unit + 3, taken)
                    taken += TT
                    unit += 4
                ahead(unit + 3)
                for g in range(3):
                    act.wait_ge(scores_ready, 11 * h + 9 + g)
                    if h and not g:
                        act.wait_ge(pv_done, h)
                    nc.scalar.activation(SX[:, g, :], ps[4 + (11 * h + 8 + g) % 2][:, :], ACT.Copy).then_inc(scores_copied, 1)
                act.wait_ge(pv_done, h + 1)
                nc.scalar.activation(OS[:, :, h * P:(h + 1) * P], BC[:, :].rearrange("p (c v) -> p c v", c=TT), ACT.Copy)\
                    .then_inc(o_copied, 1)
            unit += 6
            ahead(unit + 3)
            taken += 6
            wide_sigmoid(unit + 3, taken)
            ahead(OUT + 3)
            for b in range(TT):
                act.wait_ge(nm_ready, b + 1)
                nk = 3 if 0 < b < TT - 1 else 2
                for n in range(HQ):
                    nc.scalar.activation(S[:, n, 0:nk * P], S[:, n, 0:nk * P], ACT.Exp, bias=nm8[:, n:n + 1], scale=SCALE,
                                         accum_out=l8[:, n:n + 1]).then_inc(s_exp, 1)
                nc.scalar.activation(e8[:, :], e8[:, :], ACT.Exp).then_inc(s_soft, 1)
                for n in range(1, HQ, 2):
                    act.wait_ge(pt_ready, HQ * b + n + 1)
                    if HQ * b + n >= 2:
                        act.wait_ge(att_pv_done, HQ * b + n - 1)
                    nc.scalar.activation(PT[:, 1, 0:nk * P], ps[1][:, 0:nk * P], ACT.Copy).then_inc(pt_odd, 1)
                act.wait_ge(att_scaled, b + 1)
                nc.scalar.activation(SQ[:, b % 2, :], ATT[:, b, :], ACT.Square, accum_out=ass[:, b:b + 1]).then_inc(att_sq, 1)
            for c in range(TT):
                if c >= 2:
                    act.wait_ge(osq, c - 1)
                else:
                    act.wait_ge(att_sq, TT - 1 + c)
                nc.scalar.activation(SQ[:, c % 2, :], OS[:, c, :], ACT.Square).then_inc(achain, 1)
            act.wait_ge(att_sq, TT)
            nc.scalar.activation(aroot, ass, ACT.Sqrt, bias=eps[:, :], scale=1.0 / (HQ * DH)).then_inc(oroot_ready, 1)
            act.wait_ge(osq, TT)
            nc.scalar.activation(oroot, oss, ACT.Sqrt, bias=eps[:, :], scale=1.0 / P).then_inc(oroot_ready, 1)
            for t in range(KD):
                act.wait_ge(mix_turned, t + 1)
                nc.scalar.activation(XH[:, t, :], ps[t % 4][:, :], ACT.Copy,
                                     **(dict(scale=attgain[:, t:t + 1]) if t < 4 else {})).then_inc(mixh, 1)
            for m in range(KD):
                ahead(OUT + m + 4)
                square_y(m, 8, YM)
            root(3)
            ffn(1, FFN2)
            root(5)
            for n in range(4):
                act.wait_ge(out_turned, 2 * n + 2)
                nc.scalar.activation(xout[:, n, 512:1024], ps[2 * (n % 2) + 1][:, :], ACT.Copy).then_inc(out_copied, 1)

        @block.tensor
        def _(pe):
            def three(dst, s, k, xh, xl, first, last):
                w = slice(k * P, (k + 1) * P)
                nc.tensor.matmul(dst, WH[:, s, w], xh, start=first, stop=False)
                nc.tensor.matmul(dst, WH[:, s, w], xl, start=False, stop=False)
                return nc.tensor.matmul(dst, WL[:, s, w], xh, start=False, stop=last)

            def abreast(first, banks, e):
                for k in range(KD):
                    pe.wait_ge(xl_ready, KD * e + k + 1)
                    pe.wait_ge(xh_ready, KD * e + k + 1)
                    if k == KD - 1:
                        stat(2 * e, SSX, x_summed, KD * e + KD)
                    for u, bank in enumerate(banks):
                        if not k:
                            pe.wait_ge(lo_done, first + u + 1)
                        mm = three(bank[:, :], (first + u) % NSLOT, k, XH[:, k, :], XL[:, k, :], not k, k == KD - 1)
                        if k == KD - 1:
                            mm.then_inc(unit_used, 1)
                spread(2 * e)

            def stat(s, sums, ready, count):
                pe.wait_ge(ready, count)
                for c in range(TT):
                    mm = nc.tensor.matmul(STAT[:, c:c + 1], sums[:, c * P:(c + 1) * P], ones[:, :], start=True, stop=True)
                mm.then_inc(stat_ready, 1)

            def spread(s):
                pe.wait_ge(rt_ready, s + 1)
                for c in range(TT):
                    mm = nc.tensor.matmul(BC[:, c * P:(c + 1) * P], rt[:, s, c:c + 1].broadcast_to([P, P]), ident[:, :],
                                          start=True, stop=True)
                mm.then_inc(bc_ready, 1)

            def whole(n, quarter, bank, xh, xl, k0=0, nk=KD, first=True, last=True):
                pe.wait_ge(lo_done, quarter * NSLOT + (n + 1))
                for k in range(nk):
                    mm = three(bank[:, :], n % NSLOT, k, xh[:, k0 + k, :], xl[:, k0 + k, :],
                               first and not k, last and k == nk - 1)
                mm.then_inc(unit_used, 1)

            def ffn(f, first):
                abreast(first, ps[0:4], 2 * f)
                with pe.Fori(0, KF // 2 - 1) as i:
                    for a in range(2):
                        pe.wait_ge(up_scaled, i * 2 + (KF * f + a + 1))
                        for b in range(2):
                            whole(first + NSLOT + 2 * a + b, i, ps[2 * a + b], XH, XL)
                hh, hl = hid[f]
                with pe.Fori(0, 2) as i:
                    for m in range(4):
                        for u, (k0, nk) in enumerate(KSPLIT):
                            if m == 0:
                                pe.wait_ge(h_ready, KF * f + min(k0 + nk, KF))
                            if not u:
                                pe.wait_ge(y_copied, i * 4 + (16 * f + m + 1))
                            whole(first + N_UP + 3 * m + u, i * 3, ps[4 + m % 2], hh, hl, k0, nk, not u, u == 2)
                stat(4 * f + 1, SS, y_summed, 16 * f + KD)
                spread(4 * f + 1)

            pe.wait_ge(const_in, CONST_IN)
            nc.tensor.transpose(ps[6][:, 0:NV], vec_rows[:, :], ident[0:NV, 0:NV]).then_inc(vecs_turned, 1)
            for k in range(KD):
                if k >= 3:
                    pe.wait_ge(x_ready, k - 2)
                for c in range(TT):
                    if not k:
                        pe.wait_ge(x_in[c], 16)
                    mm = nc.tensor.transpose(turn[k % 3][:, c * P:(c + 1) * P], xin[:, c, k * P:(k + 1) * P], ident[:, :])
                mm.then_inc(x_turned, 1)
            ffn(0, FFN1)

            def wide(first, banks):
                for u in range(4):
                    pe.wait_ge(lo_done, first + u + 1)
                    s = (first + u) % NSLOT
                    for c in range(TT):
                        for kk in range(2):
                            k, w = 2 * u + kk, slice(kk * 512, (kk + 1) * 512)
                            t = slice(c * P, (c + 1) * P)
                            nc.tensor.matmul(banks[c][:, :], XH[:, k, t], WH[:, s, w], start=not k, stop=False)
                            nc.tensor.matmul(banks[c][:, :], XL[:, k, t], WH[:, s, w], start=False, stop=False)
                            mm = nc.tensor.matmul(banks[c][:, :], XH[:, k, t], WL[:, s, w], start=False, stop=k == KD - 1)
                    mm.then_inc(unit_used, 1)

            def level_side(h, lv, side):
                half = 1 << lv
                q = W[:, h % 2, 0 if side else 3, :]
                return q.rearrange("p (c b s j) -> p c b s j", c=TT, s=2, j=half)[:, :, :, side, :]

            def scores(h):
                b = h % 2

                def bank(g):
                    n = 11 * h + g
                    if n >= 2:
                        hp, gp = (n - 2) // 11, (n - 2) % 11
                        if gp < 8:
                            pe.wait_ge(scores_masked, 8 * hp + gp + 1)
                        else:
                            pe.wait_ge(scores_copied, 3 * hp + gp - 7)
                    return ps[4 + n % 2]

                pe.wait_ge(tree_ready, 9 * h + 1)
                to = bank(0)
                for c in range(TT):
                    t = slice(c * P, (c + 1) * P)
                    mm = nc.tensor.matmul(to[:, t], KS[:, b, t], Qh[:, b, t], start=True, stop=True)
                mm.then_inc(scores_ready, 1)
                for lv in range(7):
                    pe.wait_ge(tree_ready, 9 * h + 1 + lv)
                    to = bank(1 + lv)
                    for side in range(2):
                        q = level_side(h, lv, side)
                        for c in range(TT):
                            mm = nc.tensor.matmul(to[:, side * 256 + c * 64:side * 256 + (c + 1) * 64],
                                                  W[:, b, 2 if side else 1, c * P:(c + 1) * P], q[:, c], start=True, stop=True)
                    mm.then_inc(scores_ready, 1)
                pe.wait_ge(tree_ready, 9 * h + 8)
                to = bank(8)
                for c in range(TT):
                    o = c ^ 1
                    fwd = o > c
                    mm = nc.tensor.matmul(to[:, c * P:(c + 1) * P], W[:, b, 2 if fwd else 1, c * P:(c + 1) * P],
                                          W[:, b, 0 if fwd else 3, o * P:(o + 1) * P], start=True, stop=True)
                mm.then_inc(scores_ready, 1)
                pe.wait_ge(tree_ready, 9 * h + 9)
                for g in range(2):
                    to = bank(9 + g)
                    o = 256 * (1 - g)
                    for c in range(2):
                        ck = 2 * g + c
                        mm = nc.tensor.matmul(to[:, c * 256:(c + 1) * 256], W[:, b, 1 if g else 2, ck * P:(ck + 1) * P],
                                              W[:, b, 3 if g else 0, o:o + 256], start=True, stop=True)
                    mm.then_inc(scores_ready, 1)

            def values(h):
                pe.wait_ge(scores_masked, 8 * h + 8)
                pe.wait_ge(scores_copied, 3 * h + 3)
                pe.wait_ge(proj_taken, 3 + TT)
                if h:
                    pe.wait_ge(o_copied, h)
                else:
                    pe.wait_ge(rsb_ready, 2)
                for t in range(TT):
                    for n, c in enumerate(range(TT)):
                        if c == t:
                            s = SD[:, t * P:(t + 1) * P]
                        elif c == t ^ 1:
                            s = SX[:, 0, c * P:(c + 1) * P]
                        else:
                            at = (c % 2) * 256 + (t % 2) * P
                            s = SX[:, 1 + c // 2, at:at + P]
                        mm = nc.tensor.matmul(BC[:, t * P:(t + 1) * P], s, V[:, c, h * P:(h + 1) * P],
                                              start=not n, stop=n == TT - 1)
                mm.then_inc(pv_done, 1)

            abreast(MIX, ps[0:3], 1)
            unit, taken = MIX + 3, 3
            bank_at = {0: 1, 1: 2, 2: 3}

            def narrow(n, bank):
                pe.wait_ge(proj_taken, bank_at[bank])
                whole(n, 0, ps[bank], XH, XL)

            pe.wait_ge(proj_taken, 3)
            wide(unit, ps[0:4])
            unit += 4
            for b in range(4):
                bank_at[b] = 4 + b
            taken = 7
            scores(0)
            values(0)
            for h in range(1, NH):
                for t in range(3):
                    bank = (3 * (h - 1) + t) % 4
                    narrow(unit, bank)
                    unit += 1
                    taken += 1
                    bank_at[bank] = taken
                scores(h)
                values(h)

            def rotate(r, n):
                pe.wait_ge(proj_taken, TAKEN_QKV + n + 1)
                pe.wait_ge(mix_in, MIX_IN)
                if r:
                    pe.wait_ge(rope_done, r)
                nc.tensor.matmul(ps[6][:, :], swap[:, :], TMP[:, n % 2, :], start=True, stop=True).then_inc(rot_ready, 1)

            for n in range(6):
                bank = (3 * (NH - 1) + n) % 4
                narrow(unit, bank)
                unit += 1
                taken += 1
                bank_at[bank] = taken
                if n == 1:
                    pe.wait_ge(proj_taken, taken)
                    pe.wait_ge(o_copied, NH)
                    for c in range(TT):
                        mm = nc.tensor.transpose(BC[:, c * P:(c + 1) * P], TMP[:, 1, c * P:(c + 1) * P], ident[:, :])
                    mm.then_inc(va_turned, 1)
                else:
                    rotate(max(n - 1, 0), n)
            pe.wait_ge(proj_taken, taken)
            wide(unit, ps[0:4])
            unit += 4
            taken += 4

            def att_values(b, n, k0, nk):
                pe.wait_ge((pt_even, pt_odd)[n % 2], 4 * b + n // 2 + 1)
                j, kv = n // 2, n % 2
                if not n:
                    pe.wait_ge(va_ready, 1)
                    if b:
                        pe.wait_ge(att_scaled, b)
                to = BC[:, (kv * G + j) * DH:(kv * G + j + 1) * DH]
                for c in range(nk):
                    mm = nc.tensor.matmul(to, PT[:, n % 2, c * P:(c + 1) * P], VA[:, k0 + c, kv * DH:(kv + 1) * DH],
                                          start=not c, stop=c == nk - 1)
                mm.then_inc(att_pv_done, 1)

            for b in range(TT):
                k0 = max(b - 1, 0)
                nk = 3 if 0 < b < TT - 1 else 2
                pe.wait_ge(rope_done, 5)
                for n in range(HQ):
                    j, kv = n // 2, n % 2
                    r = slice(kv * DH, (kv + 1) * DH)
                    if HQ * b + n >= 2:
                        pe.wait_ge(s_max, HQ * b + n - 1)
                    nc.tensor.matmul(ps[4 + n % 2][:, 0:nk * P], qT[r, j, b * P:(b + 1) * P], kT[r, k0 * P:(k0 + nk) * P],
                                     start=True, stop=True).then_inc(s_ready, 1)
                for n in range(HQ):
                    j, kv = n // 2, n % 2
                    pe.wait_ge(s_exp, HQ * b + n + 1)
                    count = 4 * b + n // 2
                    if count:
                        pe.wait_ge((pt_even, pt_odd)[n % 2], count)
                    else:
                        pe.wait_ge(proj_taken, taken)
                    for c in range(nk):
                        mm = nc.tensor.transpose(ps[n % 2][:, c * P:(c + 1) * P], S[:, n, c * P:(c + 1) * P], ident[:, :])
                    mm.then_inc(pt_ready, 1)
                    if n:
                        att_values(b, n - 1, k0, nk)
                att_values(b, HQ - 1, k0, nk)

            for t in range(KD):
                if t < 4:
                    pe.wait_ge(mixT, 1)
                    src = ATT
                else:
                    pe.wait_ge(mixT, 2)
                    src = OS
                if t >= 4:
                    pe.wait_ge(mixl, t - 3)
                f = slice((t % 4) * P, (t % 4 + 1) * P)
                for c in range(TT):
                    mm = nc.tensor.transpose(ps[t % 4][:, c * P:(c + 1) * P], src[:, c, f], ident[:, :])
                mm.then_inc(mix_turned, 1)
            for m in range(KD):
                pe.wait_ge(mixh, KD)
                pe.wait_ge(mixl, KD)
                pe.wait_ge(y_copied, KD + m + 1)
                whole(OUT + m, 0, ps[4 + m % 2], XH, XL)
            stat(3, SS, y_summed, 2 * KD)
            spread(3)
            ffn(1, FFN2)
            for n in range(8):
                c, half = n // 2, n % 2
                pe.wait_ge(x_ready, 4 * KD)
                if n >= 4:
                    pe.wait_ge((out_copied_v, out_copied)[n % 2], (n - 4) // 2 + 1)
                for k in range(4):
                    mm = nc.tensor.transpose(ps[n % 4][:, k * P:(k + 1) * P], xT[:, 4 * half + k, c * P:(c + 1) * P], ident[:, :])
                mm.then_inc(out_turned, 1)

        @block.vector
        def _(dve):
            steps = [0]

            def step(ins):
                ins.then_inc(vchain, 1)
                steps[0] += 1
                dve.wait_ge(vchain, steps[0])

            def split_low(e, k):
                dve.wait_ge(xh_ready, KD * e + k + 1)
                nc.vector.scalar_tensor_tensor(out=XL[:, k, :], in0=xT[:, k, :], scalar=gains[:, 2 * e, k:k + 1],
                                               in1=XH[:, k, :].bitcast(fp32), op0=ALU.mult, op1=ALU.subtract).then_inc(xl_ready, 1)

            def inverse(s):
                dve.wait_ge(root_ready, s + 1)
                nc.vector.reciprocal(rt[:, s, :], rt_root[:, s, :]).then_inc(rt_ready, 1)

            def take_rms(e):
                inverse(2 * e)
                dve.wait_ge(bc_ready, 2 * e + 1)
                nc.vector.tensor_copy(RSB[:, :], BC[:, :]).then_inc(rsb_ready, 1)
                dve.wait_ge(rsb_ready, e + 1)

            def add_norm(e, buf):
                s = 2 * e - 1
                inverse(s)
                dve.wait_ge(bc_ready, s + 1)
                for k in range(KD):
                    step(nc.vector.tensor_tensor(TMP[:, k % 2, :], buf[:, k, :], BC[:, :], ALU.mult))
                    nc.vector.scalar_tensor_tensor(out=xT[:, k, :], in0=TMP[:, k % 2, :], scalar=gains[:, s, k:k + 1],
                                                   in1=xT[:, k, :], op0=ALU.mult, op1=ALU.add).then_inc(x_ready, 1)
                    if k and e < 3:
                        split_low(e, k - 1)
                if e < 3:
                    split_low(e, KD - 1)

            def clear_sum():
                step(nc.vector.memset(SS[:, :], 0.0))

            def take_y(m, used, count, buf):
                dve.wait_ge(unit_used, used)
                nc.vector.tensor_copy(buf[:, m, :], ps[4 + m % 2][:, :]).then_inc(y_copied, 1)
                if m:
                    add_square(m - 1, count)
                if m == KD - 1:
                    add_square(m, count)

            def add_square(m, count):
                dve.wait_ge(y_squared, count + m + 1)
                if m:
                    dve.wait_ge(y_summed, count + m)
                nc.vector.tensor_tensor(SS[:, :], SS[:, :], SQ[:, m % 2, :], ALU.add).then_inc(y_summed, 1)

            def ffn(f, first):
                hh, hl = hid[f]
                take_rms(2 * f)
                clear_sum()
                base = steps[0]
                with dve.Fori(0, KF // 2) as i:
                    for a in range(2):
                        n = i * 2 + (KF * f + a + 1)
                        dve.wait_ge(unit_used, i * NSLOT + (first + 2 * a + 1))
                        nc.vector.tensor_tensor(TMP[:, a, :], ps[2 * a][:, :], RSB[:, :], ALU.mult).then_inc(gate_scaled, 1)
                        dve.wait_ge(unit_used, i * NSLOT + (first + 2 * a + 2))
                        nc.vector.tensor_tensor(SQ[:, a, :], ps[2 * a + 1][:, :], RSB[:, :], ALU.mult).then_inc(up_scaled, 1)
                        dve.wait_ge(up_scaled, n)
                        nc.vector.tensor_tensor(SQ[:, a, :], SQ[:, a, :], TMP[:, a, :], ALU.mult).then_inc(vchain, 1)
                        dve.wait_ge(vchain, i * 6 + (base + 3 * a + 1))
                        dve.wait_ge(gate_sig, n)
                        nc.vector.tensor_tensor(SQ[:, a, :], SQ[:, a, :], SQX[:, a, :], ALU.mult).then_inc(vchain, 1)
                        dve.wait_ge(vchain, i * 6 + (base + 3 * a + 2))
                        j = i * 2 + a
                        nc.vector.tensor_copy(hh[:, j, :], SQ[:, a, :]).then_inc(vchain, 1)
                        dve.wait_ge(vchain, i * 6 + (base + 3 * a + 3))
                        nc.vector.tensor_tensor(hl[:, j, :], SQ[:, a, :], hh[:, j, :].bitcast(fp32), ALU.subtract).then_inc(h_ready, 1)
                steps[0] += 3 * KF
                for m in range(KD):
                    take_y(m, first + N_UP + len(KSPLIT) * (m + 1), 16 * f, YB)

            nc.vector.memset(ones[:, :], 1.0).then_inc(y_copied, 1)
            nc.vector.memset(eps[:, :], EPS).then_inc(y_copied, 1)
            dve.wait_ge(vecs_turned, 1)
            step(nc.vector.tensor_copy(vecs[:, :], ps[6][:, 0:NV]))
            nc.vector.tensor_scalar(gains[:, 1, :], gains[:, 1, :], 0.5, None, ALU.mult)
            step(nc.vector.tensor_scalar(gains[:, 5, :], gains[:, 5, :], 0.5, None, ALU.mult))
            step(nc.vector.tensor_tensor(lbm.rearrange("p (d h) -> p d h", d=2), lbr[:, :, 0, :], lbr[:, :, 1, :], ALU.max))
            nc.vector.tensor_tensor(lbr[:, :, 0, :], lbr[:, :, 0, :], lbm.rearrange("p (d h) -> p d h", d=2), ALU.subtract)
            nc.vector.tensor_tensor(lbr[:, :, 1, :], lbr[:, :, 1, :], lbm.rearrange("p (d h) -> p d h", d=2),
                                    ALU.subtract).then_inc(lb_max, 1)
            dve.wait_ge(const_in, CONST_IN)
            nc.vector.memset(small[:, 32:33], 0.0).then_inc(set_up, 1)

            for k in range(KD):
                dve.wait_ge(x_turned, k + 1)
                nc.vector.tensor_copy(xT[:, k, :], turn[k % 3][:, :]).then_inc(x_ready, 1)
                if k:
                    split_low(0, k - 1)
            split_low(0, KD - 1)
            ffn(0, FFN1)
            add_norm(1, YB)

            take_rms(1)
            clear_sum()
            dve.wait_ge(lb_exp, 1)
            step(nc.vector.tensor_tensor(lbs.rearrange("p (d h) -> p d h", d=2), lbr[:, :, 0, :], lbr[:, :, 1, :], ALU.add))
            step(nc.vector.reciprocal(lbs, lbs))
            step(nc.vector.tensor_tensor(lb.rearrange("p (d h) -> p d h", d=2), lbr[:, :, 0, :],
                                         lbs.rearrange("p (d h) -> p d h", d=2), ALU.mult))
            step(nc.vector.tensor_scalar(lb1, lb, -1.0, 1.0, ALU.mult, ALU.add))

            def gates(h, unit):
                b = h % 2
                for t in range(3):
                    n = 3 * h + t
                    dve.wait_ge(unit_used, unit + t + 1)
                    if n >= 2:
                        dve.wait_ge(proj_sig, n - 1)
                    bank = t if h == 0 else (3 * (h - 1) + t) % 4
                    nc.vector.tensor_tensor(TMP[:, n % 2, :], ps[bank][:, :], RSB[:, :], ALU.mult).then_inc(proj_taken, 1)
                dve.wait_ge(proj_sig, 3 * h + 3)
                for d in range(2):
                    at = 4 * d + h
                    step(nc.vector.tensor_scalar(Fg[:, b, d, :], Fg[:, b, d, :], lb1[:, at:at + 1], lb[:, at:at + 1], ALU.mult, ALU.add))
                if h >= 2:
                    dve.wait_ge(pv_done, h - 1)
                nc.vector.tensor_scalar(W[:, b, 2, :], Fg[:, b, 0, :], -1.0, 1.0, ALU.mult, ALU.add)
                step(nc.vector.tensor_scalar(W[:, b, 1, :], Fg[:, b, 1, :], -1.0, 1.0, ALU.mult, ALU.add))
                nc.vector.tensor_tensor(W[:, b, 0, :], Qh[:, b, :], Fg[:, b, 0, :], ALU.mult)
                nc.vector.tensor_tensor(W[:, b, 3, :], Qh[:, b, :], Fg[:, b, 1, :], ALU.mult)
                nc.vector.tensor_tensor(KS[:, b, :], W[:, b, 1, :], W[:, b, 2, :], ALU.add).then_inc(tree_ready, 1)

            GOFF = [0, 0, 256, 384, 448, 480, 496, 504, 508]

            def whole_decay(h, lv):
                if lv == 0:
                    return Fg[:, h % 2, :, :]
                return GT[:, :, GOFF[lv]:GOFF[lv] + (TOK >> lv)]

            def grow(h, lv):
                b, half = h % 2, 1 << lv
                dve.wait_ge(tree_ready, 9 * h + 1 + lv)
                g = whole_decay(h, lv).rearrange("p d (b s) -> p d b s", s=2)
                if lv < 7:
                    nc.vector.tensor_tensor(whole_decay(h, lv + 1), g[:, :, :, 0], g[:, :, :, 1], ALU.mult)
                dve.wait_ge(scores_ready, 11 * h + 2 + lv)
                for side in range(2):
                    w = W[:, b, (2, 0)[side]:(4, 2)[side], :].rearrange("p a (b s j) -> p a b s j", s=2, j=half)[:, :, :, side, :]
                    if half == 1:
                        w = w.rearrange("p a b j -> p a (b j)")
                        by = g[:, :, :, 1 - side]
                    else:
                        by = g[:, :, :, 1 - side].unsqueeze(3).broadcast_to([P, 2, TOK // (2 * half), half])
                    ins = nc.vector.tensor_tensor(w, w, by, ALU.mult)
                ins.then_inc(tree_ready, 1)

            def masked(h):
                dve.wait_ge(scores_ready, 11 * h + 1)
                if h:
                    dve.wait_ge(pv_done, h)
                nc.vector.tensor_tensor(SD[:, :].rearrange("p (c t) -> p c t", c=TT),
                                        ps[4 + 11 * h % 2][:, :].rearrange("p (c t) -> p c t", c=TT),
                                        ident[:, :].unsqueeze(1).broadcast_to([P, TT, P]), ALU.mult).then_inc(scores_masked, 1)
                for lv in range(7):
                    grow(h, lv)
                    half = 1 << lv
                    dve.wait_ge(scores_masked, 8 * h + 1 + lv)
                    nc.vector.copy_predicated(SD[:, :].rearrange("p (b s j) -> p s b j", s=2, j=half), masks[:, lv, :],
                                              ps[4 + (11 * h + 1 + lv) % 2][:, :]).then_inc(scores_masked, 1)
                grow(h, 7)

            def values_in(last, to, gain):
                dve.wait_ge(unit_used, last + 1)
                for c in range(TT):
                    dve.wait_ge(wide_sig, (TT if gain else 0) + c + 1)
                    nc.vector.scalar_tensor_tensor(out=to[:, c, :], in0=ps[c][:, :], scalar=rt[:, 2, c:c + 1],
                                                   in1=SQX[:, c % 2, :], op0=ALU.mult, op1=ALU.mult).then_inc(proj_taken, 1)

            unit = MIX
            dve.wait_ge(mix_in, MIX_IN)
            for h in range(NH):
                gates(h, unit)
                unit += 3
                if h == 0:
                    step(nc.vector.tensor_copy(masks[:, :, :], mask_in[:, :, :]))
                    values_in(unit + 3, V, False)
                    unit += 4
                masked(h)
            for n in range(6):
                dve.wait_ge(unit_used, unit + 1)
                unit += 1
                bank = (3 * (NH - 1) + n) % 4
                nc.vector.tensor_tensor(TMP[:, n % 2, :], ps[bank][:, :], RSB[:, :], ALU.mult).then_inc(proj_taken, 1)
                dve.wait_ge(proj_taken, TAKEN_QKV + n + 1)
                if n == 1:
                    dve.wait_ge(va_turned, 1)
                    nc.vector.tensor_copy(VA[:, :, :], BC[:, :].rearrange("p (c d) -> p c d", c=TT)).then_inc(va_ready, 1)
                    continue
                r = max(n - 1, 0)
                to = kT[:, :] if n == 0 else qT[:, n - 2, :]
                step(nc.vector.tensor_tensor(SQ[:, 0, :], TMP[:, n % 2, :], rope[:, 0, :], ALU.mult))
                dve.wait_ge(rot_ready, r + 1)
                step(nc.vector.tensor_tensor(to, ps[6][:, :], rope[:, 1, :], ALU.mult))
                nc.vector.tensor_tensor(to, to, SQ[:, 0, :], ALU.add).then_inc(rope_done, 1)
            values_in(unit + 3, HGATE, True)
            dve.wait_ge(proj_taken, TAKEN_QKV + 6 + TT)

            for b in range(TT):
                nk = 3 if 0 < b < TT - 1 else 2
                at = 0 if b else P
                if b:
                    dve.wait_ge(pt_ready, HQ * b)
                for n in range(HQ):
                    dve.wait_ge(s_ready, HQ * b + n + 1)
                    nc.vector.tensor_tensor_reduce(out=S[:, n, 0:nk * P], in0=ps[4 + n % 2][:, 0:nk * P],
                                                   in1=band[:, at:at + nk * P], scale=1.0, scalar=-3e38,
                                                   op0=ALU.add, op1=ALU.max, accum_out=m8[:, n:n + 1]).then_inc(s_max, 1)
                dve.wait_ge(s_max, HQ * (b + 1))
                sk = sink[:, :].rearrange("p (s j) -> p j s", s=HKV)

                def by_pair(x):
                    return x.rearrange("p (j s) -> p j s", s=HKV)

                step(nc.vector.scalar_tensor_tensor(out=by_pair(m8), in0=by_pair(m8), scalar=SCALE, in1=sk, op0=ALU.mult, op1=ALU.max))
                nc.vector.tensor_scalar(nm8, m8, -1.0, None, ALU.mult)
                nc.vector.tensor_tensor(by_pair(e8), sk, by_pair(m8), ALU.subtract).then_inc(nm_ready, 1)
                for n in range(0, HQ, 2):
                    dve.wait_ge(pt_ready, HQ * b + n + 1)
                    if HQ * b + n >= 2:
                        dve.wait_ge(att_pv_done, HQ * b + n - 1)
                    nc.vector.tensor_copy(PT[:, 0, 0:nk * P], ps[0][:, 0:nk * P]).then_inc(pt_even, 1)
                dve.wait_ge(s_soft, b + 1)
                step(nc.vector.tensor_tensor(r8, l8, e8, ALU.add))
                step(nc.vector.reciprocal(r8, r8))
                dve.wait_ge(att_pv_done, HQ * (b + 1))
                nc.vector.tensor_tensor(ATT[:, b, :].rearrange("p (s j d) -> p s j d", s=HKV, j=G),
                                        BC[:, :].rearrange("p (s j d) -> p s j d", s=HKV, j=G),
                                        r8.rearrange("p (j s) -> p s j", s=HKV).unsqueeze(3).broadcast_to([P, HKV, G, DH]),
                                        ALU.mult).then_inc(att_scaled, 1)
            for c in range(TT):
                dve.wait_ge(achain, c + 1)
                nc.vector.reduce_sum(oss[:, NH * c:NH * (c + 1)], SQ[:, c % 2, :].rearrange("p (h v) -> p h v", h=NH), AX.X).then_inc(osq, 1)
                heads = HGATE[:, c, :].rearrange("p (h v) -> p h v", h=NH)
                step(nc.vector.tensor_tensor(heads, heads, HGN[:, :].unsqueeze(1).broadcast_to([P, NH, P]), ALU.mult))
                step(nc.vector.tensor_tensor(OS[:, c, :], OS[:, c, :], HGATE[:, c, :], ALU.mult))
            dve.wait_ge(oroot_ready, 1)
            step(nc.vector.reciprocal(arr, aroot))
            for b in range(TT):
                ins = nc.vector.tensor_scalar(ATT[:, b, :], ATT[:, b, :], arr[:, b:b + 1], None, ALU.mult)
            ins.then_inc(mixT, 1)
            dve.wait_ge(oroot_ready, 2)
            step(nc.vector.reciprocal(orr, oroot))
            for c in range(TT):
                heads = OS[:, c, :].rearrange("p (h v) -> p h v", h=NH)
                ins = nc.vector.tensor_tensor(heads, heads, orr[:, NH * c:NH * (c + 1)].unsqueeze(2).broadcast_to([P, NH, P]), ALU.mult)
            ins.then_inc(mixT, 1)
            for t in range(KD):
                dve.wait_ge(mixh, t + 1)
                if t < 4:
                    nc.vector.scalar_tensor_tensor(out=XL[:, t, :], in0=ps[t % 4][:, :], scalar=attgain[:, t:t + 1],
                                                   in1=XH[:, t, :].bitcast(fp32), op0=ALU.mult, op1=ALU.subtract).then_inc(mixl, 1)
                else:
                    nc.vector.tensor_tensor(XL[:, t, :], ps[t % 4][:, :], XH[:, t, :].bitcast(fp32), ALU.subtract).then_inc(mixl, 1)
            for m in range(KD):
                take_y(m, OUT + m + 1, KD, YM)
            add_norm(2, YM)
            ffn(1, FFN2)
            add_norm(3, YB)
            for n in range(4):
                dve.wait_ge(out_turned, 2 * n + 1)
                nc.vector.tensor_copy(xout[:, n, 0:512], ps[2 * (n % 2)][:, :]).then_inc(out_copied_v, 1)


def kernel(**inputs):
    import concourse.bacc as bacc
    from concourse.bass_utils import run_bass_kernel_spmd

    nc = bacc.Bacc("TRN2", target_bir_lowering=False, num_devices=1)
    arrays = {name: np.ascontiguousarray(a) for name, a in inputs.items()}
    arrays.update(host_tables())
    io = {name: nc.dram_tensor(name, a.shape, mybir.dt.from_np(a.dtype), kind="ExternalInput").ap() for name, a in arrays.items()}
    out = nc.dram_tensor("out", (1, TOK, D), mybir.dt.float32, kind="ExternalOutput").ap()
    encoder_layer(nc, io, out)
    r = run_bass_kernel_spmd(nc, [arrays], core_ids=[0])
    return r.results[0]["out"]
```

```python
import numpy as np
import concourse.bass as bass
from concourse import mybir
from contextlib import ExitStack

P = 128
TOK = 512
D = 1024
F = 2816
KD = D // P
KF = F // P
TT = TOK // P
HQ, HKV, DH = 8, 2, 64
G = HQ // HKV
NH = 4
ROT = 16
THETA = 500000.0
WINDOW = 128
EPS = 1e-6
SCALE = DH ** -0.5
NSLOT = 4
KSPLIT = ((0, 8), (8, 7), (15, 7))
BIG = 8e30

SLOT = KD * P

C_Q, C_K, C_V = 0, 512, 640
C_HQ, C_HFF, C_HFB, C_HI, C_HG = 768, 1280, 1792, 2304, 2816

N_UP = 2 * KF
N_DOWN = len(KSPLIT) * KD
FFN1 = 0
MIX = N_UP + N_DOWN
MIX_UNITS = 26
OUT = MIX + MIX_UNITS
FFN2 = OUT + KD


def mixer_units():
    units = [("head", 0, t) for t in range(3)] + [("hi", 2 * k) for k in range(4)]
    between = [[("k",), ("v",)], [("q", 0)], [("q", 1), ("q", 2), ("q", 3)]]
    for h in range(1, NH):
        units += [("head", h, t) for t in range(3)] + between[h - 1]
    return units + [("hg", 2 * k) for k in range(4)]


def mixer_schedule():
    halves = [("half", n, p) for n in range(3 + 4, MIX_UNITS) for p in range(2)]
    units, out, late = mixer_units(), [], []

    def fill():
        late_now = late[:]
        late.clear()
        item = halves.pop(0)
        out.append(item)
        out.extend(late_now)
        if item[2] and units[item[1]][0] in "kvq":
            late.append(("turn", item[1]))

    for h in range(NH):
        for g in range(11):
            out.append(("score", h, g))
            if not g and h:
                out.append(("values", h - 1))
            if g < 9:
                fill()
    fill()
    out.append(("values", NH - 1))
    while halves:
        fill()
    assert not late
    return out


def host_tables():
    pos = np.arange(TOK, dtype=np.float32)
    half = ROT // 2
    inv = np.exp(np.float32(-np.log(THETA)) * np.arange(half, dtype=np.float32) * np.float32(2.0 / ROT)).astype(np.float32)
    ang = (pos[:, None] * inv[None, :]).astype(np.float32).astype(np.float64)
    cos = np.ones((P, TOK), np.float32)
    sin = np.zeros((P, TOK), np.float32)
    swap = np.zeros((P, P), np.float32)
    for s in range(2):
        for d in range(half):
            a, b = s * DH + d, s * DH + half + d
            cos[a] = cos[b] = np.cos(ang[:, d])
            sin[a] = sin[b] = np.sin(ang[:, d])
            swap[b, a] = -1.0
            swap[a, b] = 1.0
    ident = np.eye(P, dtype=np.float32)
    q = np.arange(P)[:, None]
    k = np.arange(3 * P)[None, :] - P
    band = np.where(np.abs(k - q) <= WINDOW, 0.0, -BIG).astype(np.float32)
    levels = []
    s = np.arange(P)
    for lv in range(7):
        h = 1 << lv
        m = np.zeros((P, 2, TT, P // (2 * h), h), np.float32)
        for side in range(2):
            for b in range(P // (2 * h)):
                hit = (s // (2 * h) == b) & ((s // h) % 2 != side)
                m[:, side, :, b, :] = hit[:, None, None]
        levels.append(m.reshape(P, TOK))
    return {
        "t_square": np.ascontiguousarray(np.concatenate([ident, swap, band], 1)),
        "t_rope": np.ascontiguousarray(np.concatenate([cos, sin], 1)),
        "t_mask": np.ascontiguousarray(np.stack(levels, 1)),
    }


def encoder_layer(nc, io, out):
    fp32, f32r, u8 = mybir.dt.float32, mybir.dt.float32r, mybir.dt.uint8
    ALU, ACT, AX = mybir.AluOpType, mybir.ActivationFunctionType, mybir.AxisListType
    ctx = ExitStack()
    with ctx:
        def sb(name, shape, dt=fp32, to=ctx):
            return to.enter_context(nc.sbuf_tensor(name, shape, dt))

        def sem(name):
            return ctx.enter_context(nc.semaphore(name))

        xT = sb("xT", [P, KD, TOK])
        raw = sb("raw", [P, NSLOT, SLOT])
        WH, WL = sb("WH", [P, NSLOT, SLOT], f32r), sb("WL", [P, NSLOT, SLOT], f32r)
        NV = 6 * KD + 4 * NH + 4
        vec_rows = sb("vec_rows", [NV, P])
        vecs = sb("vecs", [P, NV])
        gains = vecs[:, 0:6 * KD].rearrange("p (v k) -> p v k", k=KD)
        lbr = vecs[:, 6 * KD:6 * KD + 4 * NH].rearrange("p (d r h) -> p d r h", d=2, r=2)
        attgain = vecs[:, 6 * KD + 4 * NH:NV]
        sink = sb("sink", [P, HQ])
        HGN = sb("HGN", [P, P])
        small = sb("small", [P, 256])
        ident = sb("ident", [P, P])
        ones, eps = sb("ones", [P, 1]), sb("eps", [P, 1])
        rt_root, rt = sb("rt_root", [P, 6, TT]), sb("rt", [P, 6, TT])
        RSB = sb("RSB", [P, TOK])
        TMP = sb("TMP", [P, 2, TOK])
        SQ = sb("SQ", [P, 2, TOK])
        SQX = sb("SQX", [P, 2, TOK])
        SS, SSX = sb("SS", [P, TOK]), sb("SSX", [P, TOK])
        XH = sb("XH", [P, KD, TOK], f32r)
        with nc.sbuf_tensor("YB", [P, KD, TOK], fp32) as YB:
            pass
        XL = sb("XL", [P, KD, TOK], f32r)
        ps = [ctx.enter_context(nc.psum_tensor(f"ps{b}", [P, 512], fp32)) for b in range(8)]
        STAT, BC = ps[6], ps[7]
        turn = (ps[4], ps[5], ps[7])

        def place(*wanted):
            with ExitStack() as region:
                return [region.enter_context(nc.sbuf_tensor(n, s, d)) for n, s, d in wanted]

        hid = [place((f"hh{f}", [P, KF, TOK], f32r), (f"hl{f}", [P, KF, TOK], f32r)) for f in (1, 2)]
        xin, = place(("xin", [P, TT, D], fp32))
        xout, = place(("xout", [P, TT, D], fp32))
        common = [("V", [P, TT, TOK], fp32), ("OS", [P, TT, TOK], fp32), ("rope", [P, 2, TOK], fp32),
                  ("qT", [P, G, TOK], fp32), ("kT", [P, TOK], fp32), ("VA", [P, TT, P], fp32),
                  ("swap", [P, P], fp32), ("band", [P, 3 * P], fp32)]
        V, OS, rope, qT, kT, VA, swap, band, W, GT, Fg, Qh, KS, SD, SX, masks = place(
            *common, ("W", [P, 2, 4, TOK], fp32), ("GT", [P, 2, TOK], fp32), ("Fg", [P, 2, 2, TOK], fp32),
            ("Qh", [P, 2, TOK], fp32), ("KS", [P, 2, TOK], fp32), ("SD", [P, TOK], fp32),
            ("SX", [P, 3, TOK], fp32), ("masks", [P, 7, TOK], u8))
        *_, HGATE, ATT, S, PT = place(
            *[(n + "_", s, d) for n, s, d in common], ("HGATE", [P, TT, TOK], fp32), ("ATT", [P, TT, TOK], fp32),
            ("S", [P, 2, HQ, 3 * P], fp32), ("PT", [P, 2, 3 * P], fp32))
        mask_in, = place(("mask_in", [P, 7, TOK], fp32))
        YM, = place(("YM", [P, KD, TOK], fp32))
        lbm, lbs = small[:, 0:8], small[:, 8:16]
        lb, lb1 = small[:, 16:24], small[:, 24:32]
        m8, nm8, l8, e8, r8 = ([small[:, 48 + 16 * n + 8 * b:56 + 16 * n + 8 * b] for b in range(2)] for n in range(5))
        oss, oroot, orr = (small[:, 128 + 16 * n:144 + 16 * n] for n in range(3))
        ass, aroot, arr = (small[:, 176 + 4 * n:180 + 4 * n] for n in range(3))
        MIX_ORDER = [4, 5, 6, 7, 0, 1, 2, 3]
        OUT_BANK = [ps[b] for b in (4, 5, 2, 3, 0, 1, 0, 1)]
        MIX_TURN = [ps[b] for b in (0, 1, 6, 7)]

        raw_full = [sem(f"raw_full{s}") for s in range(NSLOT)]
        hi_done, lo_done = sem("hi_done"), sem("lo_done")
        unit_used = sem("unit_used")
        second_full = [sem(f"second_full{j}") for j in range(G)]
        const_in, mix_in, x_in = sem("const_in"), sem("mix_in"), [sem(f"x_in{c}") for c in range(TT)]
        CONST_IN, MIX_IN = 12 * 16, 4 * 16
        set_up = sem("set_up")
        x_turned = sem("x_turned")
        x_ready, xh_ready, xl_ready = sem("x_ready"), sem("xh_ready"), sem("xl_ready")
        x_squared, x_summed = sem("x_squared"), sem("x_summed")
        y_copied, y_squared, y_summed = sem("y_copied"), sem("y_squared"), sem("y_summed")
        stat_ready, root_ready, rt_ready, bc_ready, rsb_ready = (
            sem(n) for n in ("stat_ready", "root_ready", "rt_ready", "bc_ready", "rsb_ready"))
        gate_scaled, up_scaled, gate_sig, h_ready = (sem(n) for n in ("gate_scaled", "up_scaled", "gate_sig", "h_ready"))
        vchain, achain, pchain = sem("vchain"), sem("achain"), sem("pchain")
        proj_taken, proj_sig = sem("proj_taken"), sem("proj_sig")
        base_ready, tree_ready = sem("base_ready"), sem("tree_ready")
        scores_ready, scores_masked, scores_copied = sem("scores_ready"), sem("scores_masked"), sem("scores_copied")
        pv_done, o_copied = sem("pv_done"), sem("o_copied")
        rot_ready, rope_done, va_turned, va_ready = (sem(n) for n in ("rot_ready", "rope_done", "va_turned", "va_ready"))
        s_ready, s_max, s_exp, s_soft = (sem(n) for n in ("s_ready", "s_max", "s_exp", "s_soft"))
        pt_ready, pt_even, pt_odd, att_pv_done, att_scaled = (
            sem(n) for n in ("pt_ready", "pt_even", "pt_odd", "att_pv_done", "att_scaled"))
        nm_ready, att_sq, osq, oroot_ready, mixT, mix_turned, mixh, mixl = (
            sem(n) for n in ("nm_ready", "att_sq", "osq", "oroot_ready", "mixT", "mix_turned", "mixh", "mixl"))
        orr_ready, hg_final = sem("orr_ready"), sem("hg_final")
        wide_sig, vecs_turned = sem("wide_sig"), sem("vecs_turned")
        out_turned, out_copied, out_copied_v, stored = (sem(n) for n in ("out_turned", "out_copied", "out_copied_v", "stored"))
        lb_max, lb_exp = sem("lb_max"), sem("lb_exp")

        w_of = {s: (io[f"ffn{s}_w_gate"][0].rearrange("(k p) f -> p k f", p=P),
                    io[f"ffn{s}_w_up"][0].rearrange("(k p) f -> p k f", p=P),
                    io[f"ffn{s}_w_down"][0].rearrange("(k p) f -> p k f", p=P)) for s in (1, 2)}
        w_in = io["w_in"][0].rearrange("(k p) f -> p k f", p=P)
        w_out = io["w_out"][0].rearrange("(k p) f -> p k f", p=P)
        MIXU, SCHEDULE = mixer_units(), mixer_schedule()
        NARROW = [n for n, u in enumerate(MIXU) if u[0] not in ("hi", "hg")]
        TURNED = [n for n, u in enumerate(MIXU) if u[0] in ("k", "q")]
        HEADED = [n for n, u in enumerate(MIXU) if u[0] == "head"]

        def bank_of(n):
            i = NARROW.index(n)
            return i if i < 3 else (i - 3) % 4

        def taken(n):
            i = NARROW.index(n)
            return i + 1 + (TT if i >= 3 else 0)

        def bank_free(n):
            i = NARROW.index(n)
            return taken(NARROW[i - 4]) if i >= 7 else 3 + bank_of(n) + 1

        ALL_TAKEN = len(NARROW) + TT
        block = ctx.enter_context(nc.Block())

        def turns(n, quarter=0):
            return quarter + (n // NSLOT + 1)

        @block.sync
        def _(sp):
            def load(n, quarter, src):
                if n >= NSLOT:
                    sp.wait_ge(lo_done, quarter * NSLOT + (n - NSLOT + 1))
                nk = src.shape[1]
                dst = raw[:, n % NSLOT, 0:nk * src.shape[2]].rearrange("p (k f) -> p k f", k=nk)
                sp.dma_start(dst, src).then_inc(raw_full[n % NSLOT], 16)

            def load_pair(n, j):
                sp.wait_ge(lo_done, n - NSLOT + 1)
                dst = raw[:, n % NSLOT, :].rearrange("p (k s d) -> p s k d", k=KD, s=HKV)
                for s, full in enumerate((raw_full[n % NSLOT], second_full[j])):
                    c = C_Q + (s * G + j) * DH
                    sp.dma_start(dst[:, s], w_in[:, :, c:c + DH]).then_inc(full, 16)

            def load_ffn(s, first):
                gate, up, down = w_of[s]
                for b in range(NSLOT):
                    load(first + b, 0, (gate, up)[b % 2][:, :, (b // 2) * P:(b // 2 + 1) * P])
                with sp.Fori(0, KF // 2 - 1) as i:
                    for b in range(NSLOT):
                        load(first + NSLOT + b, i, (gate, up)[b % 2][:, :, bass.ds(i * (2 * P) + (2 + b // 2) * P, P)])
                for m in range(KD):
                    for u, (k0, nk) in enumerate(KSPLIT):
                        load(first + N_UP + len(KSPLIT) * m + u, 0, down[:, k0:k0 + nk, m * P:(m + 1) * P])

            row = 0
            for name in ("ffn1_pre_norm", "ffn1_post_norm", "mix_pre_norm", "mix_post_norm", "ffn2_pre_norm", "ffn2_post_norm"):
                sp.dma_start(vec_rows[row:row + KD, :], io[name][0].rearrange("(k p) -> k p", p=P)).then_inc(const_in, 16)
                row += KD
            for name in ("hgrn_lb_fwd", "hgrn_lb_bwd"):
                sp.dma_start(vec_rows[row:row + 2 * NH, :], io[name].rearrange("r (h p) -> (r h) p", p=P)).then_inc(const_in, 16)
                row += 2 * NH
            sp.dma_start(vec_rows[row:row + 4, :], io["attn_out_norm"][0].rearrange("(k p) -> k p", p=P)).then_inc(const_in, 16)
            sp.dma_start(ident[:, :], io["t_square"][:, 0:P]).then_inc(const_in, 16)
            sp.dma_start(sink[:, :], io["attn_sink"][0].partition_broadcast(P)).then_inc(const_in, 16)
            sp.dma_start(HGN[:, :], io["hgrn_out_norm"][0].partition_broadcast(P)).then_inc(const_in, 16)
            for c in range(TT):
                sp.dma_start(xin[:, c, :], io["x"][0, c * P:(c + 1) * P, :]).then_inc(x_in[c], 16)
            load_ffn(1, FFN1)
            for u, unit in enumerate(MIXU):
                if u == 0:
                    sp.wait_ge(unit_used, MIX)
                    sp.dma_start(mask_in[:, :, :], io["t_mask"]).then_inc(mix_in, 16)
                    sp.dma_start(rope[:, :, :], io["t_rope"].rearrange("p (a t) -> p a t", a=2)).then_inc(mix_in, 16)
                    sp.dma_start(swap[:, :], io["t_square"][:, P:2 * P]).then_inc(mix_in, 16)
                    sp.dma_start(band[:, :], io["t_square"][:, 2 * P:5 * P]).then_inc(mix_in, 16)
                if unit[0] == "q":
                    load_pair(MIX + u, unit[1])
                elif unit[0] in ("hi", "hg"):
                    c = C_HI if unit[0] == "hi" else C_HG
                    load(MIX + u, 0, w_in[:, unit[1]:unit[1] + 2, c:c + 4 * P])
                else:
                    c = (C_HQ, C_HFF, C_HFB)[unit[2]] + unit[1] * P if unit[0] == "head" else {"k": C_K, "v": C_V}[unit[0]]
                    load(MIX + u, 0, w_in[:, :, c:c + P])
            for m in range(KD):
                load(OUT + m, 0, w_out[:, :, m * P:(m + 1) * P])
            load_ffn(2, FFN2)
            sp.wait_ge(out_copied, 4)
            sp.wait_ge(out_copied_v, 4)
            sp.dma_start(out[0].rearrange("(c p) d -> p c d", p=P), xout[:, :, :]).then_inc(stored, 16)
            sp.wait_ge(stored, 16)

        @block.gpsimd
        def _(pool):
            def lo(n, quarter, size):
                pool.wait_ge(hi_done, quarter * NSLOT + (n + 1))
                s = n % NSLOT
                pool.tensor_tensor(WL[:, s, 0:size], raw[:, s, 0:size], WH[:, s, 0:size].bitcast(fp32),
                                   ALU.subtract).then_inc(lo_done, 1)

            def sum_x(e):
                if e:
                    pool.wait_ge(stat_ready, 2 * e)
                pool.memset(SSX[:, :], 0.0).then_inc(pchain, 1)
                pool.wait_ge(pchain, (0, 1, 2 * TT + 2)[e] + 1)
                for k in range(KD):
                    pool.wait_ge(x_squared, KD * e + k + 1)
                    if k:
                        pool.wait_ge(x_summed, KD * e + k)
                    pool.tensor_tensor(SSX[:, :], SSX[:, :], SQX[:, k % 2, :], ALU.add).then_inc(x_summed, 1)

            def lo_ffn(first, e):
                for b in range(NSLOT):
                    lo(first + b, 0, SLOT)
                sum_x(e)
                with pool.Fori(0, KF // 2 - 1) as i:
                    for b in range(NSLOT):
                        lo(first + NSLOT + b, i, SLOT)
                with pool.Fori(0, 2) as i:
                    for u in range(4 * len(KSPLIT)):
                        lo(first + N_UP + u, i * 3, KSPLIT[u % 3][1] * P)

            lo_ffn(FFN1, 0)
            for u in range(4):
                lo(MIX + u, 0, SLOT)
            sum_x(1)
            for u in range(4, MIX_UNITS + 4):
                lo(MIX + u, 0, SLOT)
            for c in range(TT):
                heads = HGATE[:, c, :].rearrange("p (h v) -> p h v", h=NH)
                pool.wait_ge(proj_taken, ALL_TAKEN + c + 1)
                pool.tensor_tensor(heads, heads, HGN[:, :].unsqueeze(1).broadcast_to([P, NH, P]), ALU.mult).then_inc(pchain, 1)
                pool.wait_ge(pchain, 3 + 2 * c)
                pool.wait_ge(achain, c + 1)
                pool.tensor_tensor(OS[:, c, :], OS[:, c, :], HGATE[:, c, :], ALU.mult).then_inc(pchain, 1)
            pool.wait_ge(orr_ready, 1)
            for c in range(TT):
                pool.wait_ge(pchain, 4 + 2 * c)
                heads = OS[:, c, :].rearrange("p (h v) -> p h v", h=NH)
                by = orr[:, NH * c:NH * (c + 1)].unsqueeze(2).broadcast_to([P, NH, P])
                pool.tensor_tensor(heads, heads, by, ALU.mult).then_inc(hg_final, 1)
            for u in range(4, KD):
                lo(OUT + u, 0, SLOT)
            lo_ffn(FFN2, 2)

        @block.scalar
        def _(act):
            def hi(n, quarter=0, size=SLOT):
                act.wait_ge(raw_full[n % NSLOT], turns(n, quarter) * 16)
                if MIX <= n < OUT and MIXU[n - MIX][0] == "q":
                    act.wait_ge(second_full[MIXU[n - MIX][1]], 16)
                if n >= NSLOT:
                    act.wait_ge(unit_used, quarter * NSLOT + (n - NSLOT + 1))
                s = n % NSLOT
                nc.scalar.activation(WH[:, s, 0:size], raw[:, s, 0:size], ACT.Copy).then_inc(hi_done, 1)

            def unit_size(n):
                for f in (FFN1, FFN2):
                    if f + N_UP <= n < f + N_UP + N_DOWN:
                        return KSPLIT[(n - f - N_UP) % 3][1] * P
                return SLOT

            done = [0]

            def ahead(n):
                while done[0] <= min(n, FFN2 + N_UP + N_DOWN - 1):
                    hi(done[0], 0, unit_size(done[0]))
                    done[0] += 1

            def root(s):
                act.wait_ge(stat_ready, s + 1)
                nc.scalar.activation(rt_root[:, s, :], STAT[:, 0:TT], ACT.Sqrt, bias=eps[:, :], scale=1.0 / D).then_inc(root_ready, 1)

            def split_high(e, k):
                act.wait_ge(x_ready, KD * e + k + 1)
                if e < 3:
                    if not k and e:
                        act.wait_ge(unit_used, (FFN1 + N_UP + N_DOWN, OUT + KD)[e - 1])
                    nc.scalar.activation(XH[:, k, :], xT[:, k, :], ACT.Copy, scale=gains[:, 2 * e, k:k + 1]).then_inc(xh_ready, 1)
                    if k >= 2:
                        act.wait_ge(x_summed, KD * e + k - 1)
                    nc.scalar.activation(SQX[:, k % 2, :], xT[:, k, :], ACT.Square).then_inc(x_squared, 1)

            def square_y(m, count, buf):
                act.wait_ge(y_copied, count + m + 3)
                if m >= 2 or count:
                    act.wait_ge(y_summed, count + m - 1)
                nc.scalar.activation(SQ[:, m % 2, :], buf[:, m, :], ACT.Square).then_inc(y_squared, 1)

            def ffn(f, first):
                for k in range(KD):
                    split_high(2 * f, k)
                root(4 * f)

                def sig(j, a):
                    act.wait_ge(gate_scaled, j)
                    nc.scalar.activation(SQX[:, a, :], TMP[:, a, :], ACT.Sigmoid).then_inc(gate_sig, 1)

                with act.Fori(0, KF // 2 - 1) as i:
                    for a in range(2):
                        for b in range(2):
                            hi(first + NSLOT + 2 * a + b, i)
                        sig(i * 2 + (KF * f + a + 1), a)
                done[0] = first + N_UP
                for a in range(2):
                    ahead(first + N_UP + 2 * a + 1)
                    sig(KF * f + KF - 2 + a + 1, a)
                for m in range(KD):
                    ahead(first + N_UP + 3 * m + 6)
                    square_y(m, 16 * f, YB)

            ahead(3)
            act.wait_ge(set_up, 1)
            ffn(0, FFN1)
            root(1)
            act.wait_ge(lb_max, 1)
            nc.scalar.activation(lbr, lbr, ACT.Exp).then_inc(lb_exp, 1)
            for k in range(KD):
                split_high(1, k)
            root(2)

            nsig = [0]

            def wide_sigmoid(used, before):
                act.wait_ge(unit_used, used)
                for c in range(TT):
                    if c >= 2:
                        act.wait_ge(proj_taken, before + c - 1)
                    nc.scalar.activation(SQX[:, c % 2, :], ps[c][:, :], ACT.Sigmoid, scale=rt[:, 2, c:c + 1]).then_inc(wide_sig, 1)

            def head_sigmoid(n):
                h, t = MIXU[n][1:]
                act.wait_ge(proj_taken, taken(n))
                nc.scalar.activation(Qh[:, h % 2, :] if t == 0 else Fg[:, h % 2, t - 1, :], TMP[:, NARROW.index(n) % 2, :],
                                     ACT.Sigmoid).then_inc(proj_sig, 1)

            ahead(MIX + 3)
            for n in range(3):
                ahead(MIX + n + 3)
                head_sigmoid(n)
            ahead(MIX + 3 + 4 + 2)
            wide_sigmoid(MIX + 3 + 4, 3)
            at = 3 + 4
            for what, n, g in (x + (0,) if len(x) == 2 else x for x in SCHEDULE):
                ahead(MIX + at + 3)
                if what == "half" and g:
                    at = n + 1
                    if MIXU[n][0] == "head":
                        head_sigmoid(n)
                elif what == "score" and g >= 8:
                    act.wait_ge(scores_ready, 11 * n + 1 + g)
                    if n:
                        act.wait_ge(pv_done, n)
                    nc.scalar.activation(SX[:, g - 8, :], ps[4 + (11 * n + g) % 2][:, :], ACT.Copy).then_inc(scores_copied, 1)
                elif what == "values":
                    act.wait_ge(pv_done, n + 1)
                    nc.scalar.activation(OS[:, :, n * P:(n + 1) * P], BC[:, :].rearrange("p (c v) -> p c v", c=TT), ACT.Copy)\
                        .then_inc(o_copied, 1)
            ahead(OUT + 2)
            wide_sigmoid(OUT, ALL_TAKEN)
            ahead(OUT + 3)
            for c in range(TT):
                act.wait_ge(o_copied, NH)
                if c >= 2:
                    act.wait_ge(osq, c - 1)
                nc.scalar.activation(SQ[:, c % 2, :], OS[:, c, :], ACT.Square).then_inc(achain, 1)
            act.wait_ge(osq, TT)
            nc.scalar.activation(oroot, oss, ACT.Sqrt, bias=eps[:, :], scale=1.0 / P).then_inc(oroot_ready, 1)

            for b in range(TT + 1):
                if b < TT:
                    act.wait_ge(nm_ready, b + 1)
                for n in range(HQ):
                    if b < TT:
                        nk = 3 if 0 < b < TT - 1 else 2
                        w = S[:, b % 2, n, 0:nk * P]
                        nc.scalar.activation(w, w, ACT.Exp, bias=nm8[b % 2][:, n:n + 1], scale=SCALE,
                                             accum_out=l8[b % 2][:, n:n + 1]).then_inc(s_exp, 1)
                        if n == HQ - 1:
                            nc.scalar.activation(e8[b % 2], e8[b % 2], ACT.Exp).then_inc(s_soft, 1)
                    if b and n % 2:
                        c = b - 1
                        nk = 3 if 0 < c < TT - 1 else 2
                        act.wait_ge(pt_ready, HQ * c + n + 1)
                        if HQ * c + n >= 2:
                            act.wait_ge(att_pv_done, HQ * c + n - 1)
                        nc.scalar.activation(PT[:, 1, 0:nk * P], ps[1][:, 0:nk * P], ACT.Copy).then_inc(pt_odd, 1)
                if b:
                    act.wait_ge(att_scaled, b)
                    nc.scalar.activation(SQ[:, b % 2, :], ATT[:, b - 1, :], ACT.Square, accum_out=ass[:, b - 1:b]).then_inc(att_sq, 1)
            act.wait_ge(att_sq, TT)
            nc.scalar.activation(aroot, ass, ACT.Sqrt, bias=eps[:, :], scale=1.0 / (HQ * DH)).then_inc(oroot_ready, 1)
            for i, t in enumerate(MIX_ORDER):
                act.wait_ge(mix_turned, i + 1)
                nc.scalar.activation(XH[:, t, :], MIX_TURN[t % 4][:, :], ACT.Copy,
                                     **(dict(scale=attgain[:, t:t + 1]) if t < 4 else {})).then_inc(mixh, 1)
            for m in range(KD):
                ahead(OUT + m + 4)
                square_y(m, 8, YM)
            root(3)
            ffn(1, FFN2)
            root(5)
            for n in range(4):
                act.wait_ge(out_turned, 2 * n + 2)
                nc.scalar.activation(xout[:, n, 512:1024], ps[2 * (n % 2) + 1][:, :], ACT.Copy).then_inc(out_copied, 1)

        @block.tensor
        def _(pe):
            def three(dst, s, k, xh, xl, first, last):
                w = slice(k * P, (k + 1) * P)
                nc.tensor.matmul(dst, WH[:, s, w], xh, start=first, stop=False)
                nc.tensor.matmul(dst, WH[:, s, w], xl, start=False, stop=False)
                return nc.tensor.matmul(dst, WL[:, s, w], xh, start=False, stop=last)

            def abreast(first, banks, e):
                for k in range(KD):
                    pe.wait_ge(xl_ready, KD * e + k + 1)
                    pe.wait_ge(xh_ready, KD * e + k + 1)
                    if k == KD - 1:
                        stat(2 * e, SSX, x_summed, KD * e + KD)
                    for u, bank in enumerate(banks):
                        if not k:
                            pe.wait_ge(lo_done, first + u + 1)
                        mm = three(bank[:, :], (first + u) % NSLOT, k, XH[:, k, :], XL[:, k, :], not k, k == KD - 1)
                        if k == KD - 1:
                            mm.then_inc(unit_used, 1)
                spread(2 * e)

            def stat(s, sums, ready, count):
                pe.wait_ge(ready, count)
                for c in range(TT):
                    mm = nc.tensor.matmul(STAT[:, c:c + 1], sums[:, c * P:(c + 1) * P], ones[:, :], start=True, stop=True)
                mm.then_inc(stat_ready, 1)

            def spread(s):
                pe.wait_ge(rt_ready, s + 1)
                for c in range(TT):
                    mm = nc.tensor.matmul(BC[:, c * P:(c + 1) * P], rt[:, s, c:c + 1].broadcast_to([P, P]), ident[:, :],
                                          start=True, stop=True)
                mm.then_inc(bc_ready, 1)

            def half(n, bank, p):
                if not p:
                    pe.wait_ge(lo_done, n + 1)
                for k in range(KD // 2 * p, KD // 2 * (p + 1)):
                    mm = three(bank[:, :], n % NSLOT, k, XH[:, k, :], XL[:, k, :], not k, k == KD - 1)
                if p:
                    mm.then_inc(unit_used, 1)

            def whole(n, quarter, bank, xh, xl, k0=0, nk=KD, first=True, last=True):
                pe.wait_ge(lo_done, quarter * NSLOT + (n + 1))
                for k in range(nk):
                    mm = three(bank[:, :], n % NSLOT, k, xh[:, k0 + k, :], xl[:, k0 + k, :],
                               first and not k, last and k == nk - 1)
                mm.then_inc(unit_used, 1)

            def ffn(f, first):
                abreast(first, ps[0:4], 2 * f)
                with pe.Fori(0, KF // 2 - 1) as i:
                    for a in range(2):
                        pe.wait_ge(up_scaled, i * 2 + (KF * f + a + 1))
                        for b in range(2):
                            whole(first + NSLOT + 2 * a + b, i, ps[2 * a + b], XH, XL)
                hh, hl = hid[f]
                with pe.Fori(0, 2) as i:
                    for m in range(4):
                        for u, (k0, nk) in enumerate(KSPLIT):
                            if m == 0:
                                pe.wait_ge(h_ready, KF * f + min(k0 + nk, KF))
                            if not u:
                                pe.wait_ge(y_copied, i * 4 + (16 * f + m + 1))
                            whole(first + N_UP + 3 * m + u, i * 3, ps[4 + m % 2], hh, hl, k0, nk, not u, u == 2)
                stat(4 * f + 1, SS, y_summed, 16 * f + KD)
                spread(4 * f + 1)

            pe.wait_ge(const_in, CONST_IN)
            nc.tensor.transpose(ps[6][:, 0:NV], vec_rows[:, :], ident[0:NV, 0:NV]).then_inc(vecs_turned, 1)
            for k in range(KD):
                if k >= 3:
                    pe.wait_ge(x_ready, k - 2)
                for c in range(TT):
                    if not k:
                        pe.wait_ge(x_in[c], 16)
                    mm = nc.tensor.transpose(turn[k % 3][:, c * P:(c + 1) * P], xin[:, c, k * P:(k + 1) * P], ident[:, :])
                mm.then_inc(x_turned, 1)
            ffn(0, FFN1)

            def wide(n, k0, cs):
                s = n % NSLOT
                for c in cs:
                    for kk in range(2):
                        k, w, t = k0 + kk, slice(kk * 512, (kk + 1) * 512), slice(c * P, (c + 1) * P)
                        nc.tensor.matmul(ps[c][:, :], XH[:, k, t], WH[:, s, w], start=not k, stop=False)
                        nc.tensor.matmul(ps[c][:, :], XL[:, k, t], WH[:, s, w], start=False, stop=False)
                        mm = nc.tensor.matmul(ps[c][:, :], XH[:, k, t], WL[:, s, w], start=False, stop=k == KD - 1)
                if TT - 1 in cs:
                    mm.then_inc(unit_used, 1)

            def level_side(h, lv, side):
                half = 1 << lv
                q = W[:, h % 2, 0 if side else 3, :]
                return q.rearrange("p (c b s j) -> p c b s j", c=TT, s=2, j=half)[:, :, :, side, :]

            def scores(h, g):
                b, n = h % 2, 11 * h + g
                if n >= 2:
                    hp, gp = (n - 2) // 11, (n - 2) % 11
                    if gp < 8:
                        pe.wait_ge(scores_masked, 8 * hp + gp + 1)
                    else:
                        pe.wait_ge(scores_copied, 3 * hp + gp - 7)
                to = ps[4 + n % 2]
                if g < 2:
                    pe.wait_ge(base_ready, h + 1)
                else:
                    pe.wait_ge(tree_ready, 8 * h + min(g - 1, 8))
                if g == 0:
                    for c in range(TT):
                        t = slice(c * P, (c + 1) * P)
                        mm = nc.tensor.matmul(to[:, t], KS[:, b, t], Qh[:, b, t], start=True, stop=True)
                elif g < 8:
                    for side in range(2):
                        q = level_side(h, g - 1, side)
                        for c in range(TT):
                            mm = nc.tensor.matmul(to[:, side * 256 + c * 64:side * 256 + (c + 1) * 64],
                                                  W[:, b, 2 if side else 1, c * P:(c + 1) * P], q[:, c], start=True, stop=True)
                elif g == 8:
                    for c in range(TT):
                        o = c ^ 1
                        fwd = o > c
                        mm = nc.tensor.matmul(to[:, c * P:(c + 1) * P], W[:, b, 2 if fwd else 1, c * P:(c + 1) * P],
                                              W[:, b, 0 if fwd else 3, o * P:(o + 1) * P], start=True, stop=True)
                else:
                    back = g - 9
                    o = 256 * (1 - back)
                    for c in range(2):
                        ck = 2 * back + c
                        mm = nc.tensor.matmul(to[:, c * 256:(c + 1) * 256], W[:, b, 1 if back else 2, ck * P:(ck + 1) * P],
                                              W[:, b, 3 if back else 0, o:o + 256], start=True, stop=True)
                mm.then_inc(scores_ready, 1)

            def values(h):
                pe.wait_ge(scores_masked, 8 * h + 8)
                pe.wait_ge(scores_copied, 3 * h + 3)
                pe.wait_ge(proj_taken, 3 + TT)
                if h:
                    pe.wait_ge(o_copied, h)
                    if h > 1:
                        pe.wait_ge(va_ready, 1)
                else:
                    pe.wait_ge(rsb_ready, 2)
                for t in range(TT):
                    for n, c in enumerate(range(TT)):
                        if c == t:
                            s = SD[:, t * P:(t + 1) * P]
                        elif c == t ^ 1:
                            s = SX[:, 0, c * P:(c + 1) * P]
                        else:
                            at = (c % 2) * 256 + (t % 2) * P
                            s = SX[:, 1 + c // 2, at:at + P]
                        mm = nc.tensor.matmul(BC[:, t * P:(t + 1) * P], s, V[:, c, h * P:(h + 1) * P],
                                              start=not n, stop=n == TT - 1)
                mm.then_inc(pv_done, 1)

            def turn_unit(n):
                pe.wait_ge(proj_taken, taken(n))
                tmp = TMP[:, NARROW.index(n) % 2, :]
                if MIXU[n][0] == "v":
                    pe.wait_ge(o_copied, 1)
                    for c in range(TT):
                        mm = nc.tensor.transpose(BC[:, c * P:(c + 1) * P], tmp[:, c * P:(c + 1) * P], ident[:, :])
                    mm.then_inc(va_turned, 1)
                else:
                    r = TURNED.index(n)
                    pe.wait_ge(mix_in, MIX_IN)
                    if r:
                        pe.wait_ge(rope_done, r)
                    nc.tensor.matmul(ps[6][:, :], swap[:, :], tmp, start=True, stop=True).then_inc(rot_ready, 1)

            abreast(MIX, ps[0:3], 1)
            pe.wait_ge(proj_taken, 3)
            for u in range(4):
                pe.wait_ge(lo_done, MIX + 3 + u + 1)
                wide(MIX + 3 + u, 2 * u, range(TT))
            for what, n, g in (x + (0,) if len(x) == 2 else x for x in SCHEDULE):
                if what == "score":
                    scores(n, g)
                elif what == "values":
                    values(n)
                elif what == "turn":
                    turn_unit(n)
                elif MIXU[n][0] == "hg":
                    if not g:
                        pe.wait_ge(proj_taken, ALL_TAKEN)
                        pe.wait_ge(lo_done, MIX + n + 1)
                    wide(MIX + n, MIXU[n][1], (0, 1) if not g else (2, 3))
                else:
                    if not g:
                        pe.wait_ge(proj_taken, bank_free(n))
                    half(MIX + n, ps[bank_of(n)], g)

            def att_values(b, n, k0, nk):
                pe.wait_ge((pt_even, pt_odd)[n % 2], 4 * b + n // 2 + 1)
                j, kv = n // 2, n % 2
                if not n:
                    pe.wait_ge(va_ready, 1)
                    if b:
                        pe.wait_ge(att_scaled, b)
                to = BC[:, (kv * G + j) * DH:(kv * G + j + 1) * DH]
                for c in range(nk):
                    mm = nc.tensor.matmul(to, PT[:, n % 2, c * P:(c + 1) * P], VA[:, k0 + c, kv * DH:(kv + 1) * DH],
                                          start=not c, stop=c == nk - 1)
                mm.then_inc(att_pv_done, 1)

            def att_scores(b):
                k0 = max(b - 1, 0)
                nk = 3 if 0 < b < TT - 1 else 2
                for n in range(HQ):
                    j, kv = n // 2, n % 2
                    r = slice(kv * DH, (kv + 1) * DH)
                    if HQ * b + n >= 2:
                        pe.wait_ge(s_max, HQ * b + n - 1)
                    nc.tensor.matmul(ps[4 + n % 2][:, 0:nk * P], qT[r, j, b * P:(b + 1) * P], kT[r, k0 * P:(k0 + nk) * P],
                                     start=True, stop=True).then_inc(s_ready, 1)

            def att_turn(b):
                k0 = max(b - 1, 0)
                nk = 3 if 0 < b < TT - 1 else 2
                for n in range(HQ):
                    pe.wait_ge(s_exp, HQ * b + n + 1)
                    if 4 * b + n // 2:
                        pe.wait_ge((pt_even, pt_odd)[n % 2], 4 * b + n // 2)
                    else:
                        pe.wait_ge(proj_taken, ALL_TAKEN + TT)
                    for c in range(nk):
                        mm = nc.tensor.transpose(ps[n % 2][:, c * P:(c + 1) * P], S[:, b % 2, n, c * P:(c + 1) * P], ident[:, :])
                    mm.then_inc(pt_ready, 1)
                    if n:
                        att_values(b, n - 1, k0, nk)
                att_values(b, HQ - 1, k0, nk)

            pe.wait_ge(rope_done, len(TURNED))
            pe.wait_ge(scores_copied, 3 * NH)
            att_scores(0)
            for b in range(TT):
                if b + 1 < TT:
                    att_scores(b + 1)
                att_turn(b)

            def mix_turn(i, t):
                if i >= 4:
                    pe.wait_ge(mixl, i - 3)
                if i == 3:
                    pe.wait_ge(att_scaled, TT)
                src = ATT if t < 4 else OS
                f = slice((t % 4) * P, (t % 4 + 1) * P)
                for c in range(TT):
                    mm = nc.tensor.transpose(MIX_TURN[t % 4][:, c * P:(c + 1) * P], src[:, c, f], ident[:, :])
                mm.then_inc(mix_turned, 1)

            def out_products(i, t):
                pe.wait_ge(mixl, i + 1)
                for m in range(4):
                    if not i:
                        pe.wait_ge(lo_done, OUT + m + 1)
                    mm = three(OUT_BANK[m][:, :], (OUT + m) % NSLOT, t, XH[:, t, :], XL[:, t, :], not i, i == KD - 1)
                    if i == KD - 1:
                        mm.then_inc(unit_used, 1)

            pe.wait_ge(hg_final, TT)
            pe.wait_ge(pt_even, HQ // 2 * TT)
            pe.wait_ge(pt_odd, HQ // 2 * TT)
            for i, t in enumerate(MIX_ORDER[0:4]):
                mix_turn(i, t)
            for i, t in enumerate(MIX_ORDER[0:4]):
                out_products(i, t)
            pe.wait_ge(mixT, 1)
            for i, t in enumerate(MIX_ORDER[4:8]):
                mix_turn(4 + i, t)
            for i, t in enumerate(MIX_ORDER[4:8]):
                out_products(4 + i, t)
            for m in range(4, KD):
                if m >= 6:
                    pe.wait_ge(y_copied, KD + m + 1)
                else:
                    pe.wait_ge(mixl, KD)
                whole(OUT + m, 0, OUT_BANK[m], XH, XL)
            stat(3, SS, y_summed, 2 * KD)
            spread(3)
            ffn(1, FFN2)
            for n in range(8):
                c, half = n // 2, n % 2
                pe.wait_ge(x_ready, 4 * KD)
                if n >= 4:
                    pe.wait_ge((out_copied_v, out_copied)[n % 2], (n - 4) // 2 + 1)
                for k in range(4):
                    mm = nc.tensor.transpose(ps[n % 4][:, k * P:(k + 1) * P], xT[:, 4 * half + k, c * P:(c + 1) * P], ident[:, :])
                mm.then_inc(out_turned, 1)

        @block.vector
        def _(dve):
            steps = [0]

            def step(ins):
                ins.then_inc(vchain, 1)
                steps[0] += 1
                dve.wait_ge(vchain, steps[0])

            def split_low(e, k):
                dve.wait_ge(xh_ready, KD * e + k + 1)
                nc.vector.scalar_tensor_tensor(out=XL[:, k, :], in0=xT[:, k, :], scalar=gains[:, 2 * e, k:k + 1],
                                               in1=XH[:, k, :].bitcast(fp32), op0=ALU.mult, op1=ALU.subtract).then_inc(xl_ready, 1)

            def inverse(s):
                dve.wait_ge(root_ready, s + 1)
                nc.vector.reciprocal(rt[:, s, :], rt_root[:, s, :]).then_inc(rt_ready, 1)

            def take_rms(e):
                inverse(2 * e)
                dve.wait_ge(bc_ready, 2 * e + 1)
                nc.vector.tensor_copy(RSB[:, :], BC[:, :]).then_inc(rsb_ready, 1)
                dve.wait_ge(rsb_ready, e + 1)

            def add_norm(e, buf):
                s = 2 * e - 1
                inverse(s)
                dve.wait_ge(bc_ready, s + 1)
                for k in range(KD):
                    step(nc.vector.tensor_tensor(TMP[:, k % 2, :], buf[:, k, :], BC[:, :], ALU.mult))
                    nc.vector.scalar_tensor_tensor(out=xT[:, k, :], in0=TMP[:, k % 2, :], scalar=gains[:, s, k:k + 1],
                                                   in1=xT[:, k, :], op0=ALU.mult, op1=ALU.add).then_inc(x_ready, 1)
                    if k and e < 3:
                        split_low(e, k - 1)
                if e < 3:
                    split_low(e, KD - 1)

            def clear_sum():
                step(nc.vector.memset(SS[:, :], 0.0))

            def take_y(m, used, count, buf, bank=None):
                dve.wait_ge(unit_used, used)
                bank = bank or ps[4 + m % 2]
                nc.vector.tensor_copy(buf[:, m, :], bank[:, :]).then_inc(y_copied, 1)
                if m:
                    add_square(m - 1, count)
                if m == KD - 1:
                    add_square(m, count)

            def add_square(m, count):
                dve.wait_ge(y_squared, count + m + 1)
                if m:
                    dve.wait_ge(y_summed, count + m)
                nc.vector.tensor_tensor(SS[:, :], SS[:, :], SQ[:, m % 2, :], ALU.add).then_inc(y_summed, 1)

            def ffn(f, first):
                hh, hl = hid[f]
                take_rms(2 * f)
                clear_sum()
                base = steps[0]
                with dve.Fori(0, KF // 2) as i:
                    for a in range(2):
                        n = i * 2 + (KF * f + a + 1)
                        dve.wait_ge(unit_used, i * NSLOT + (first + 2 * a + 1))
                        nc.vector.tensor_tensor(TMP[:, a, :], ps[2 * a][:, :], RSB[:, :], ALU.mult).then_inc(gate_scaled, 1)
                        dve.wait_ge(unit_used, i * NSLOT + (first + 2 * a + 2))
                        nc.vector.tensor_tensor(SQ[:, a, :], ps[2 * a + 1][:, :], RSB[:, :], ALU.mult).then_inc(up_scaled, 1)
                        dve.wait_ge(up_scaled, n)
                        nc.vector.tensor_tensor(SQ[:, a, :], SQ[:, a, :], TMP[:, a, :], ALU.mult).then_inc(vchain, 1)
                        dve.wait_ge(vchain, i * 6 + (base + 3 * a + 1))
                        dve.wait_ge(gate_sig, n)
                        nc.vector.tensor_tensor(SQ[:, a, :], SQ[:, a, :], SQX[:, a, :], ALU.mult).then_inc(vchain, 1)
                        dve.wait_ge(vchain, i * 6 + (base + 3 * a + 2))
                        j = i * 2 + a
                        nc.vector.tensor_copy(hh[:, j, :], SQ[:, a, :]).then_inc(vchain, 1)
                        dve.wait_ge(vchain, i * 6 + (base + 3 * a + 3))
                        nc.vector.tensor_tensor(hl[:, j, :], SQ[:, a, :], hh[:, j, :].bitcast(fp32), ALU.subtract).then_inc(h_ready, 1)
                steps[0] += 3 * KF
                for m in range(KD):
                    take_y(m, first + N_UP + len(KSPLIT) * (m + 1), 16 * f, YB)

            nc.vector.memset(ones[:, :], 1.0).then_inc(y_copied, 1)
            nc.vector.memset(eps[:, :], EPS).then_inc(y_copied, 1)
            dve.wait_ge(vecs_turned, 1)
            step(nc.vector.tensor_copy(vecs[:, :], ps[6][:, 0:NV]))
            nc.vector.tensor_scalar(gains[:, 1, :], gains[:, 1, :], 0.5, None, ALU.mult)
            step(nc.vector.tensor_scalar(gains[:, 5, :], gains[:, 5, :], 0.5, None, ALU.mult))
            step(nc.vector.tensor_tensor(lbm.rearrange("p (d h) -> p d h", d=2), lbr[:, :, 0, :], lbr[:, :, 1, :], ALU.max))
            nc.vector.tensor_tensor(lbr[:, :, 0, :], lbr[:, :, 0, :], lbm.rearrange("p (d h) -> p d h", d=2), ALU.subtract)
            nc.vector.tensor_tensor(lbr[:, :, 1, :], lbr[:, :, 1, :], lbm.rearrange("p (d h) -> p d h", d=2),
                                    ALU.subtract).then_inc(lb_max, 1)
            dve.wait_ge(const_in, CONST_IN)
            nc.vector.memset(small[:, 32:33], 0.0).then_inc(set_up, 1)

            for k in range(KD):
                dve.wait_ge(x_turned, k + 1)
                nc.vector.tensor_copy(xT[:, k, :], turn[k % 3][:, :]).then_inc(x_ready, 1)
                if k:
                    split_low(0, k - 1)
            split_low(0, KD - 1)
            ffn(0, FFN1)
            add_norm(1, YB)

            take_rms(1)
            clear_sum()
            dve.wait_ge(lb_exp, 1)
            step(nc.vector.tensor_tensor(lbs.rearrange("p (d h) -> p d h", d=2), lbr[:, :, 0, :], lbr[:, :, 1, :], ALU.add))
            step(nc.vector.reciprocal(lbs, lbs))
            step(nc.vector.tensor_tensor(lb.rearrange("p (d h) -> p d h", d=2), lbr[:, :, 0, :],
                                         lbs.rearrange("p (d h) -> p d h", d=2), ALU.mult))
            step(nc.vector.tensor_scalar(lb1, lb, -1.0, 1.0, ALU.mult, ALU.add))

            def scale_unit(n):
                i = NARROW.index(n)
                dve.wait_ge(unit_used, MIX + n + 1)
                if i >= 2:
                    last = NARROW[i - 2]
                    if MIXU[last][0] == "head":
                        dve.wait_ge(proj_sig, HEADED.index(last) + 1)
                    elif MIXU[last][0] == "v":
                        dve.wait_ge(va_turned, 1)
                    else:
                        dve.wait_ge(rot_ready, TURNED.index(last) + 1)
                nc.vector.tensor_tensor(TMP[:, i % 2, :], ps[bank_of(n)][:, :], RSB[:, :], ALU.mult).then_inc(proj_taken, 1)

            def gates(h):
                b = h % 2
                dve.wait_ge(proj_sig, 3 * h + 3)
                for d in range(2):
                    at = 4 * d + h
                    step(nc.vector.tensor_scalar(Fg[:, b, d, :], Fg[:, b, d, :], lb1[:, at:at + 1], lb[:, at:at + 1], ALU.mult, ALU.add))
                if h >= 2:
                    dve.wait_ge(pv_done, h - 1)
                nc.vector.tensor_scalar(W[:, b, 2, :], Fg[:, b, 0, :], -1.0, 1.0, ALU.mult, ALU.add)
                step(nc.vector.tensor_scalar(W[:, b, 1, :], Fg[:, b, 1, :], -1.0, 1.0, ALU.mult, ALU.add))
                nc.vector.tensor_tensor(W[:, b, 0, :], Qh[:, b, :], Fg[:, b, 0, :], ALU.mult)
                nc.vector.tensor_tensor(W[:, b, 3, :], Qh[:, b, :], Fg[:, b, 1, :], ALU.mult)
                nc.vector.tensor_tensor(KS[:, b, :], W[:, b, 1, :], W[:, b, 2, :], ALU.add).then_inc(base_ready, 1)

            GOFF = [0, 0, 256, 384, 448, 480, 496, 504, 508]

            def whole_decay(h, lv):
                if lv == 0:
                    return Fg[:, h % 2, :, :]
                return GT[:, :, GOFF[lv]:GOFF[lv] + (TOK >> lv)]

            def grow(h, lv):
                b, half = h % 2, 1 << lv
                if lv:
                    dve.wait_ge(tree_ready, 8 * h + lv)
                else:
                    dve.wait_ge(base_ready, h + 1)
                g = whole_decay(h, lv).rearrange("p d (b s) -> p d b s", s=2)
                if lv < 7:
                    nc.vector.tensor_tensor(whole_decay(h, lv + 1), g[:, :, :, 0], g[:, :, :, 1], ALU.mult)
                dve.wait_ge(scores_ready, 11 * h + 2 + lv)
                for side in range(2):
                    w = W[:, b, (2, 0)[side]:(4, 2)[side], :].rearrange("p a (b s j) -> p a b s j", s=2, j=half)[:, :, :, side, :]
                    if half == 1:
                        w = w.rearrange("p a b j -> p a (b j)")
                        by = g[:, :, :, 1 - side]
                    else:
                        by = g[:, :, :, 1 - side].unsqueeze(3).broadcast_to([P, 2, TOK // (2 * half), half])
                    ins = nc.vector.tensor_tensor(w, w, by, ALU.mult)
                ins.then_inc(tree_ready, 1)

            def diagonal(h):
                dve.wait_ge(scores_ready, 11 * h + 1)
                if h:
                    dve.wait_ge(pv_done, h)
                nc.vector.tensor_tensor(SD[:, :].rearrange("p (c t) -> p c t", c=TT),
                                        ps[4 + 11 * h % 2][:, :].rearrange("p (c t) -> p c t", c=TT),
                                        ident[:, :].unsqueeze(1).broadcast_to([P, TT, P]), ALU.mult).then_inc(scores_masked, 1)

            def take_level(h, lv):
                half = 1 << lv
                dve.wait_ge(scores_masked, 8 * h + 1 + lv)
                nc.vector.copy_predicated(SD[:, :].rearrange("p (b s j) -> p s b j", s=2, j=half), masks[:, lv, :],
                                          ps[4 + (11 * h + 1 + lv) % 2][:, :]).then_inc(scores_masked, 1)

            def values_in(used, to, gain):
                dve.wait_ge(unit_used, used)
                for c in range(TT):
                    dve.wait_ge(wide_sig, (TT if gain else 0) + c + 1)
                    nc.vector.scalar_tensor_tensor(out=to[:, c, :], in0=ps[c][:, :], scalar=rt[:, 2, c:c + 1],
                                                   in1=SQX[:, c % 2, :], op0=ALU.mult, op1=ALU.mult).then_inc(proj_taken, 1)

            def turned(n):
                if MIXU[n][0] == "v":
                    dve.wait_ge(va_turned, 1)
                    nc.vector.tensor_copy(VA[:, :, :], BC[:, :].rearrange("p (c d) -> p c d", c=TT)).then_inc(va_ready, 1)
                    return
                dve.wait_ge(proj_taken, taken(n))
                to = kT[:, :] if MIXU[n][0] == "k" else qT[:, MIXU[n][1], :]
                step(nc.vector.tensor_tensor(SQ[:, 0, :], TMP[:, NARROW.index(n) % 2, :], rope[:, 0, :], ALU.mult))
                dve.wait_ge(rot_ready, TURNED.index(n) + 1)
                step(nc.vector.tensor_tensor(to, ps[6][:, :], rope[:, 1, :], ALU.mult))
                nc.vector.tensor_tensor(to, to, SQ[:, 0, :], ALU.add).then_inc(rope_done, 1)

            dve.wait_ge(mix_in, MIX_IN)
            for n in range(3):
                scale_unit(n)
            gates(0)
            step(nc.vector.tensor_copy(masks[:, :, :], mask_in[:, :, :]))
            values_in(MIX + 3 + 4, V, False)
            for what, n, g in (x + (0,) if len(x) == 2 else x for x in SCHEDULE):
                if what == "score":
                    if g == 0:
                        diagonal(n)
                    elif g < 8:
                        grow(n, g - 1)
                        take_level(n, g - 1)
                    elif g == 8:
                        grow(n, 7)
                elif what == "turn":
                    turned(n)
                elif what == "half" and g and n in NARROW:
                    scale_unit(n)
                    if MIXU[n][0] == "head" and MIXU[n][2] == 2:
                        gates(MIXU[n][1])
            values_in(OUT, HGATE, True)
            for c in range(TT):
                dve.wait_ge(achain, c + 1)
                nc.vector.reduce_sum(oss[:, NH * c:NH * (c + 1)], SQ[:, c % 2, :].rearrange("p (h v) -> p h v", h=NH), AX.X).then_inc(osq, 1)
            dve.wait_ge(proj_taken, ALL_TAKEN + TT)

            def by_pair(x):
                return x.rearrange("p (j s) -> p j s", s=HKV)

            def att_max(b):
                nk = 3 if 0 < b < TT - 1 else 2
                at, e = 0 if b else P, b % 2
                if b >= 2:
                    dve.wait_ge(pt_ready, HQ * (b - 1))
                for n in range(HQ):
                    dve.wait_ge(s_ready, HQ * b + n + 1)
                    nc.vector.tensor_tensor_reduce(out=S[:, e, n, 0:nk * P], in0=ps[4 + n % 2][:, 0:nk * P],
                                                   in1=band[:, at:at + nk * P], scale=1.0, scalar=-3e38,
                                                   op0=ALU.add, op1=ALU.max, accum_out=m8[e][:, n:n + 1]).then_inc(s_max, 1)
                dve.wait_ge(s_max, HQ * (b + 1))
                sk = sink[:, :].rearrange("p (s j) -> p j s", s=HKV)
                step(nc.vector.scalar_tensor_tensor(out=by_pair(m8[e]), in0=by_pair(m8[e]), scalar=SCALE, in1=sk, op0=ALU.mult, op1=ALU.max))
                nc.vector.tensor_scalar(nm8[e], m8[e], -1.0, None, ALU.mult)
                nc.vector.tensor_tensor(by_pair(e8[e]), sk, by_pair(m8[e]), ALU.subtract).then_inc(nm_ready, 1)

            def att_take(b):
                nk = 3 if 0 < b < TT - 1 else 2
                e = b % 2
                for n in range(0, HQ, 2):
                    dve.wait_ge(pt_ready, HQ * b + n + 1)
                    if HQ * b + n >= 2:
                        dve.wait_ge(att_pv_done, HQ * b + n - 1)
                    nc.vector.tensor_copy(PT[:, 0, 0:nk * P], ps[0][:, 0:nk * P]).then_inc(pt_even, 1)
                dve.wait_ge(s_soft, b + 1)
                step(nc.vector.tensor_tensor(r8[e], l8[e], e8[e], ALU.add))
                step(nc.vector.reciprocal(r8[e], r8[e]))
                dve.wait_ge(att_pv_done, HQ * (b + 1))
                nc.vector.tensor_tensor(ATT[:, b, :].rearrange("p (s j d) -> p s j d", s=HKV, j=G),
                                        BC[:, :].rearrange("p (s j d) -> p s j d", s=HKV, j=G),
                                        r8[e].rearrange("p (j s) -> p s j", s=HKV).unsqueeze(3).broadcast_to([P, HKV, G, DH]),
                                        ALU.mult).then_inc(att_scaled, 1)

            att_max(0)
            dve.wait_ge(oroot_ready, 1)
            nc.vector.reciprocal(orr, oroot).then_inc(orr_ready, 1)
            for b in range(TT):
                if b + 1 < TT:
                    att_max(b + 1)
                att_take(b)
            for i, t in enumerate(MIX_ORDER):
                if i == 4:
                    dve.wait_ge(oroot_ready, 2)
                    step(nc.vector.reciprocal(arr, aroot))
                    for b in range(TT):
                        ins = nc.vector.tensor_scalar(ATT[:, b, :], ATT[:, b, :], arr[:, b:b + 1], None, ALU.mult)
                    ins.then_inc(mixT, 1)
                dve.wait_ge(mixh, i + 1)
                if t < 4:
                    nc.vector.scalar_tensor_tensor(out=XL[:, t, :], in0=MIX_TURN[t % 4][:, :], scalar=attgain[:, t:t + 1],
                                                   in1=XH[:, t, :].bitcast(fp32), op0=ALU.mult, op1=ALU.subtract).then_inc(mixl, 1)
                else:
                    nc.vector.tensor_tensor(XL[:, t, :], MIX_TURN[t % 4][:, :], XH[:, t, :].bitcast(fp32), ALU.subtract).then_inc(mixl, 1)
            for m in range(KD):
                take_y(m, OUT + m + 1, KD, YM, OUT_BANK[m])
            add_norm(2, YM)
            ffn(1, FFN2)
            add_norm(3, YB)
            for n in range(4):
                dve.wait_ge(out_turned, 2 * n + 1)
                nc.vector.tensor_copy(xout[:, n, 0:512], ps[2 * (n % 2)][:, :]).then_inc(out_copied_v, 1)


def kernel(**inputs):
    import concourse.bacc as bacc
    from concourse.bass_utils import run_bass_kernel_spmd

    nc = bacc.Bacc("TRN2", target_bir_lowering=False, num_devices=1)
    arrays = {name: np.ascontiguousarray(a) for name, a in inputs.items()}
    arrays.update(host_tables())
    io = {name: nc.dram_tensor(name, a.shape, mybir.dt.from_np(a.dtype), kind="ExternalInput").ap() for name, a in arrays.items()}
    out = nc.dram_tensor("out", (1, TOK, D), mybir.dt.float32, kind="ExternalOutput").ap()
    encoder_layer(nc, io, out)
    r = run_bass_kernel_spmd(nc, [arrays], core_ids=[0])
    return r.results[0]["out"]
```

```python
import numpy as np
import concourse.bass as bass
from concourse import mybir
from contextlib import ExitStack

P = 128
TOK = 512
D = 1024
F = 2816
KD = D // P
KF = F // P
TT = TOK // P
HQ, HKV, DH = 8, 2, 64
G = HQ // HKV
NH = 4
ROT = 16
THETA = 500000.0
WINDOW = 128
EPS = 1e-6
SCALE = DH ** -0.5
NSLOT = 4
KSPLIT = ((0, 8), (8, 7), (15, 7))
BIG = 8e30

SLOT = KD * P

C_Q, C_K, C_V = 0, 512, 640
C_HQ, C_HFF, C_HFB, C_HI, C_HG = 768, 1280, 1792, 2304, 2816

N_UP = 2 * KF
N_DOWN = len(KSPLIT) * KD
FFN1 = 0
MIX = N_UP + N_DOWN
MIX_UNITS = 26
OUT = MIX + MIX_UNITS
FFN2 = OUT + KD


def mixer_units():
    units = [("head", 0, t) for t in range(3)] + [("hi", 2 * k) for k in range(4)]
    between = [[("k",), ("v",)], [("q", 0)], [("q", 1), ("q", 2), ("q", 3)]]
    for h in range(1, NH):
        units += [("head", h, t) for t in range(3)] + between[h - 1]
    return units + [("hg", 2 * k) for k in range(4)]


def mixer_schedule():
    halves = [("half", n, p) for n in range(3 + 4, MIX_UNITS) for p in range(2)]
    units, out, late = mixer_units(), [], []

    def fill():
        late_now = late[:]
        late.clear()
        item = halves.pop(0)
        out.append(item)
        out.extend(late_now)
        if item[2] and units[item[1]][0] in "kvq":
            late.append(("turn", item[1]))

    for h in range(NH):
        for g in range(11):
            out.append(("score", h, g))
            if not g and h:
                out.append(("values", h - 1))
            if g < 9:
                fill()
    fill()
    out.append(("values", NH - 1))
    while halves:
        fill()
    assert not late
    return out


def host_tables():
    pos = np.arange(TOK, dtype=np.float32)
    half = ROT // 2
    inv = np.exp(np.float32(-np.log(THETA)) * np.arange(half, dtype=np.float32) * np.float32(2.0 / ROT)).astype(np.float32)
    ang = (pos[:, None] * inv[None, :]).astype(np.float32).astype(np.float64)
    cos = np.ones((P, TOK), np.float32)
    sin = np.zeros((P, TOK), np.float32)
    swap = np.zeros((P, P), np.float32)
    for s in range(2):
        for d in range(half):
            a, b = s * DH + d, s * DH + half + d
            cos[a] = cos[b] = np.cos(ang[:, d])
            sin[a] = sin[b] = np.sin(ang[:, d])
            swap[b, a] = -1.0
            swap[a, b] = 1.0
    ident = np.eye(P, dtype=np.float32)
    q = np.arange(P)[:, None]
    k = np.arange(3 * P)[None, :] - P
    band = np.where(np.abs(k - q) <= WINDOW, 0.0, -BIG).astype(np.float32)
    levels = []
    s = np.arange(P)
    for lv in range(7):
        h = 1 << lv
        m = np.zeros((P, 2, TT, P // (2 * h), h), np.float32)
        for side in range(2):
            for b in range(P // (2 * h)):
                hit = (s // (2 * h) == b) & ((s // h) % 2 != side)
                m[:, side, :, b, :] = hit[:, None, None]
        levels.append(m.reshape(P, TOK))
    return {
        "t_square": np.ascontiguousarray(np.concatenate([ident, swap, band], 1)),
        "t_rope": np.ascontiguousarray(np.concatenate([cos, sin], 1)),
        "t_mask": np.ascontiguousarray(np.stack(levels, 1)),
    }


def encoder_layer(nc, io, out):
    fp32, f32r, u8 = mybir.dt.float32, mybir.dt.float32r, mybir.dt.uint8
    ALU, ACT, AX = mybir.AluOpType, mybir.ActivationFunctionType, mybir.AxisListType
    ctx = ExitStack()
    with ctx:
        def sb(name, shape, dt=fp32, to=ctx):
            return to.enter_context(nc.sbuf_tensor(name, shape, dt))

        def sem(name):
            return ctx.enter_context(nc.semaphore(name))

        xT = sb("xT", [P, KD, TOK])
        raw = sb("raw", [P, NSLOT, SLOT])
        WH, WL = sb("WH", [P, NSLOT, SLOT], f32r), sb("WL", [P, NSLOT, SLOT], f32r)
        NV = 6 * KD + 4 * NH + 4
        vec_rows = sb("vec_rows", [NV, P])
        vecs = sb("vecs", [P, NV])
        gains = vecs[:, 0:6 * KD].rearrange("p (v k) -> p v k", k=KD)
        lbr = vecs[:, 6 * KD:6 * KD + 4 * NH].rearrange("p (d r h) -> p d r h", d=2, r=2)
        attgain = vecs[:, 6 * KD + 4 * NH:NV]
        sink = sb("sink", [P, HQ])
        HGN = sb("HGN", [P, P])
        small = sb("small", [P, 256])
        ident = sb("ident", [P, P])
        ones, eps = sb("ones", [P, 1]), sb("eps", [P, 1])
        rt_root, rt = sb("rt_root", [P, 6, TT]), sb("rt", [P, 6, TT])
        RSB = sb("RSB", [P, TOK])
        TMP = sb("TMP", [P, 2, TOK])
        SQ = sb("SQ", [P, 2, TOK])
        SQX = sb("SQX", [P, 2, TOK])
        SS, SSX = sb("SS", [P, TOK]), sb("SSX", [P, TOK])
        XH = sb("XH", [P, KD, TOK], f32r)
        with nc.sbuf_tensor("YB", [P, KD, TOK], fp32) as YB:
            pass
        XL = sb("XL", [P, KD, TOK], f32r)
        ps = [ctx.enter_context(nc.psum_tensor(f"ps{b}", [P, 512], fp32)) for b in range(8)]
        STAT, BC = ps[6], ps[7]
        turn = (ps[4], ps[5], ps[7])

        def place(*wanted):
            with ExitStack() as region:
                return [region.enter_context(nc.sbuf_tensor(n, s, d)) for n, s, d in wanted]

        hid = [place((f"hh{f}", [P, KF, TOK], f32r), (f"hl{f}", [P, KF, TOK], f32r)) for f in (1, 2)]
        xin, = place(("xin", [P, TT, D], fp32))
        xout, = place(("xout", [P, TT, D], fp32))
        common = [("V", [P, TT, TOK], fp32), ("OS", [P, TT, TOK], fp32), ("rope", [P, 2, TOK], fp32),
                  ("qT", [P, G, TOK], fp32), ("kT", [P, TOK], fp32), ("VA", [P, TT, P], fp32),
                  ("swap", [P, P], fp32), ("band", [P, 3 * P], fp32)]
        V, OS, rope, qT, kT, VA, swap, band, W, GT, Fg, Qh, KS, SD, SX, masks = place(
            *common, ("W", [P, 2, 4, TOK], fp32), ("GT", [P, 2, TOK], fp32), ("Fg", [P, 2, 2, TOK], fp32),
            ("Qh", [P, 2, TOK], fp32), ("KS", [P, 2, TOK], fp32), ("SD", [P, TOK], fp32),
            ("SX", [P, 3, TOK], fp32), ("masks", [P, 7, TOK], u8))
        *_, HGATE, ATT, S, PT = place(
            *[(n + "_", s, d) for n, s, d in common], ("HGATE", [P, TT, TOK], fp32), ("ATT", [P, TT, TOK], fp32),
            ("S", [P, 2, HQ, 3 * P], fp32), ("PT", [P, 2, 3 * P], fp32))
        mask_in, = place(("mask_in", [P, 7, TOK], fp32))
        YM, = place(("YM", [P, KD, TOK], fp32))
        lbm, lbs = small[:, 0:8], small[:, 8:16]
        lb, lb1 = small[:, 16:24], small[:, 24:32]
        m8, nm8, l8, e8, r8 = ([small[:, 48 + 16 * n + 8 * b:56 + 16 * n + 8 * b] for b in range(2)] for n in range(5))
        oss, oroot, orr = (small[:, 128 + 16 * n:144 + 16 * n] for n in range(3))
        ass, aroot, arr = (small[:, 176 + 4 * n:180 + 4 * n] for n in range(3))
        MIX_ORDER = [4, 5, 6, 7, 0, 1, 2, 3]
        OUT_BANK = [ps[b] for b in (2, 3, 4, 5, 0, 1, 0, 1)]
        BACK = [[ps[b] for b in (0, 1, 2, 3)], [ps[b] for b in (4, 5, 6, 0)]]

        raw_full = [sem(f"raw_full{s}") for s in range(NSLOT)]
        hi_done, lo_done = sem("hi_done"), sem("lo_done")
        unit_used = sem("unit_used")
        second_full = [sem(f"second_full{j}") for j in range(G)]
        const_in, mix_in, x_in = sem("const_in"), sem("mix_in"), [sem(f"x_in{c}") for c in range(TT)]
        CONST_IN, MIX_IN = 11 * 16, 4 * 16
        ident_in, set_up = sem("ident_in"), sem("set_up")
        lo_first = sem("lo_first")
        x_turned = sem("x_turned")
        x_ready, xh_ready, xl_ready = sem("x_ready"), sem("xh_ready"), sem("xl_ready")
        x_squared, x_summed = sem("x_squared"), sem("x_summed")
        y_copied, y_squared, y_summed = sem("y_copied"), sem("y_squared"), sem("y_summed")
        stat_ready, root_ready, rt_ready, bc_ready, rsb_ready = (
            sem(n) for n in ("stat_ready", "root_ready", "rt_ready", "bc_ready", "rsb_ready"))
        gate_scaled, up_scaled, gate_sig, h_ready = (sem(n) for n in ("gate_scaled", "up_scaled", "gate_sig", "h_ready"))
        vchain, achain, pchain = sem("vchain"), sem("achain"), sem("pchain")
        proj_taken, proj_sig = sem("proj_taken"), sem("proj_sig")
        base_ready, tree_ready = sem("base_ready"), sem("tree_ready")
        scores_ready, scores_masked, scores_copied = sem("scores_ready"), sem("scores_masked"), sem("scores_copied")
        pv_done, o_copied = sem("pv_done"), sem("o_copied")
        rot_ready, rope_done, va_turned, va_ready = (sem(n) for n in ("rot_ready", "rope_done", "va_turned", "va_ready"))
        s_ready, s_max, s_exp, s_soft = (sem(n) for n in ("s_ready", "s_max", "s_exp", "s_soft"))
        s_norm = sem("s_norm")
        pt_ready, pt_even, pt_odd, att_pv_done, att_copied = (
            sem(n) for n in ("pt_ready", "pt_even", "pt_odd", "att_pv_done", "att_copied"))
        nm_ready, att_sq, osq, oroot_ready, mix_turned, mixh, mixl = (
            sem(n) for n in ("nm_ready", "att_sq", "osq", "oroot_ready", "mix_turned", "mixh", "mixl"))
        att_sum, att_stat, aroot_ready, arr_ready, att_bc, att_tmp = (
            sem(n) for n in ("att_sum", "att_stat", "aroot_ready", "arr_ready", "att_bc", "att_tmp"))
        orr_ready, hg_final = sem("orr_ready"), sem("hg_final")
        wide_sig, vecs_turned = sem("wide_sig"), sem("vecs_turned")
        out_turned, out_copied, out_copied_v, stored = (sem(n) for n in ("out_turned", "out_copied", "out_copied_v", "stored"))
        lb_max, lb_exp = sem("lb_max"), sem("lb_exp")

        w_of = {s: (io[f"ffn{s}_w_gate"][0].rearrange("(k p) f -> p k f", p=P),
                    io[f"ffn{s}_w_up"][0].rearrange("(k p) f -> p k f", p=P),
                    io[f"ffn{s}_w_down"][0].rearrange("(k p) f -> p k f", p=P)) for s in (1, 2)}
        w_in = io["w_in"][0].rearrange("(k p) f -> p k f", p=P)
        w_out = io["w_out"][0].rearrange("(k p) f -> p k f", p=P)
        MIXU, SCHEDULE = mixer_units(), mixer_schedule()
        NARROW = [n for n, u in enumerate(MIXU) if u[0] not in ("hi", "hg")]
        TURNED = [n for n, u in enumerate(MIXU) if u[0] in ("k", "q")]
        HEADED = [n for n, u in enumerate(MIXU) if u[0] == "head"]

        def bank_of(n):
            i = NARROW.index(n)
            return i if i < 3 else (i - 3) % 4

        def taken(n):
            i = NARROW.index(n)
            return i + 1 + (TT if i >= 3 else 0)

        def bank_free(n):
            i = NARROW.index(n)
            return taken(NARROW[i - 4]) if i >= 7 else 3 + bank_of(n) + 1

        ALL_TAKEN = len(NARROW) + TT
        block = ctx.enter_context(nc.Block())

        def turns(n, quarter=0):
            return quarter + (n // NSLOT + 1)

        @block.sync
        def _(sp):
            def load(n, quarter, src):
                if n >= NSLOT:
                    sp.wait_ge(lo_done, quarter * NSLOT + (n - NSLOT + 1))
                nk = src.shape[1]
                dst = raw[:, n % NSLOT, 0:nk * src.shape[2]].rearrange("p (k f) -> p k f", k=nk)
                sp.dma_start(dst, src).then_inc(raw_full[n % NSLOT], 16)

            def load_pair(n, j):
                sp.wait_ge(lo_done, n - NSLOT + 1)
                dst = raw[:, n % NSLOT, :].rearrange("p (k s d) -> p s k d", k=KD, s=HKV)
                for s, full in enumerate((raw_full[n % NSLOT], second_full[j])):
                    c = C_Q + (s * G + j) * DH
                    sp.dma_start(dst[:, s], w_in[:, :, c:c + DH]).then_inc(full, 16)

            def load_ffn(s, first):
                gate, up, down = w_of[s]
                for b in range(NSLOT):
                    load(first + b, 0, (gate, up)[b % 2][:, :, (b // 2) * P:(b // 2 + 1) * P])
                with sp.Fori(0, KF // 2 - 1) as i:
                    for b in range(NSLOT):
                        load(first + NSLOT + b, i, (gate, up)[b % 2][:, :, bass.ds(i * (2 * P) + (2 + b // 2) * P, P)])
                for m in range(KD):
                    for u, (k0, nk) in enumerate(KSPLIT):
                        load(first + N_UP + len(KSPLIT) * m + u, 0, down[:, k0:k0 + nk, m * P:(m + 1) * P])

            sp.dma_start(ident[:, :], io["t_square"][:, 0:P]).then_inc(ident_in, 16)
            for c in range(TT):
                sp.dma_start(xin[:, c, :], io["x"][0, c * P:(c + 1) * P, :]).then_inc(x_in[c], 16)
            load_ffn(1, FFN1)
            for u, unit in enumerate(MIXU):
                if u == NSLOT:
                    sp.wait_ge(unit_used, MIX)
                    sp.dma_start(mask_in[:, :, :], io["t_mask"]).then_inc(mix_in, 16)
                    sp.dma_start(rope[:, :, :], io["t_rope"].rearrange("p (a t) -> p a t", a=2)).then_inc(mix_in, 16)
                    sp.dma_start(swap[:, :], io["t_square"][:, P:2 * P]).then_inc(mix_in, 16)
                    sp.dma_start(band[:, :], io["t_square"][:, 2 * P:5 * P]).then_inc(mix_in, 16)
                if unit[0] == "q":
                    load_pair(MIX + u, unit[1])
                elif unit[0] in ("hi", "hg"):
                    c = C_HI if unit[0] == "hi" else C_HG
                    load(MIX + u, 0, w_in[:, unit[1]:unit[1] + 2, c:c + 4 * P])
                else:
                    c = (C_HQ, C_HFF, C_HFB)[unit[2]] + unit[1] * P if unit[0] == "head" else {"k": C_K, "v": C_V}[unit[0]]
                    load(MIX + u, 0, w_in[:, :, c:c + P])
            for m in range(KD):
                load(OUT + m, 0, w_out[:, :, m * P:(m + 1) * P])
            load_ffn(2, FFN2)
            for half, c, copied, count in ((0, 0, out_copied, 1), (0, 1, out_copied, 2), (0, 2, out_copied, 3), (0, 3, out_copied, 4),
                                           (1, 0, out_copied_v, 1), (1, 1, out_copied, 5), (1, 2, out_copied_v, 2), (1, 3, out_copied, 6)):
                sp.wait_ge(copied, count)
                f = slice(half * 512, (half + 1) * 512)
                sp.dma_start(out[0, c * P:(c + 1) * P, f], xout[:, c, f]).then_inc(stored, 16)
            sp.wait_ge(stored, 8 * 16)

        @block.gpsimd
        def _(pool):
            def lo(n, quarter, size):
                pool.wait_ge(hi_done, quarter * NSLOT + (n + 1))
                s = n % NSLOT
                if n == 2:
                    pool.wait_ge(lo_first, 2)
                pool.tensor_tensor(WL[:, s, 0:size], raw[:, s, 0:size], WH[:, s, 0:size].bitcast(fp32),
                                   ALU.subtract).then_inc(lo_done, 3 if n == 2 else 1)

            def sum_x(e):
                if e:
                    pool.wait_ge(stat_ready, 2 * e)
                pool.memset(SSX[:, :], 0.0).then_inc(pchain, 1)
                pool.wait_ge(pchain, (0, 1, 2 * TT + 2)[e] + 1)
                for k in range(KD):
                    pool.wait_ge(x_squared, KD * e + k + 1)
                    if k:
                        pool.wait_ge(x_summed, KD * e + k)
                    pool.tensor_tensor(SSX[:, :], SSX[:, :], SQX[:, k % 2, :], ALU.add).then_inc(x_summed, 1)

            def lo_ffn(first, e):
                for b in range(0 if e else 2, NSLOT):
                    lo(first + b, 0, SLOT)
                sum_x(e)
                with pool.Fori(0, KF // 2 - 1) as i:
                    for b in range(NSLOT):
                        lo(first + NSLOT + b, i, SLOT)
                with pool.Fori(0, 2) as i:
                    for u in range(4 * len(KSPLIT)):
                        lo(first + N_UP + u, i * 3, KSPLIT[u % 3][1] * P)

            lo_ffn(FFN1, 0)
            for u in range(4):
                lo(MIX + u, 0, SLOT)
            sum_x(1)
            for u in range(4, MIX_UNITS + 4):
                lo(MIX + u, 0, SLOT)
            for c in range(TT):
                heads = HGATE[:, c, :].rearrange("p (h v) -> p h v", h=NH)
                pool.wait_ge(proj_taken, ALL_TAKEN + c + 1)
                pool.tensor_tensor(heads, heads, HGN[:, :].unsqueeze(1).broadcast_to([P, NH, P]), ALU.mult).then_inc(pchain, 1)
                pool.wait_ge(pchain, 3 + 2 * c)
                pool.wait_ge(achain, c + 1)
                pool.tensor_tensor(OS[:, c, :], OS[:, c, :], HGATE[:, c, :], ALU.mult).then_inc(pchain, 1)
            pool.wait_ge(orr_ready, 1)
            for c in range(TT):
                pool.wait_ge(pchain, 4 + 2 * c)
                heads = OS[:, c, :].rearrange("p (h v) -> p h v", h=NH)
                by = orr[:, NH * c:NH * (c + 1)].unsqueeze(2).broadcast_to([P, NH, P])
                pool.tensor_tensor(heads, heads, by, ALU.mult).then_inc(hg_final, 1)
            for u in range(4, KD):
                lo(OUT + u, 0, SLOT)
            lo_ffn(FFN2, 2)

        @block.scalar
        def _(act):
            def hi(n, quarter=0, size=SLOT):
                act.wait_ge(raw_full[n % NSLOT], turns(n, quarter) * 16)
                if MIX <= n < OUT and MIXU[n - MIX][0] == "q":
                    act.wait_ge(second_full[MIXU[n - MIX][1]], 16)
                if n >= NSLOT:
                    act.wait_ge(unit_used, quarter * NSLOT + (n - NSLOT + 1))
                s = n % NSLOT
                nc.scalar.activation(WH[:, s, 0:size], raw[:, s, 0:size], ACT.Copy).then_inc(hi_done, 1)

            def unit_size(n):
                for f in (FFN1, FFN2):
                    if f + N_UP <= n < f + N_UP + N_DOWN:
                        return KSPLIT[(n - f - N_UP) % 3][1] * P
                return SLOT

            done = [0]

            def ahead(n):
                while done[0] <= min(n, FFN2 + N_UP + N_DOWN - 1):
                    hi(done[0], 0, unit_size(done[0]))
                    done[0] += 1

            def root(s):
                act.wait_ge(stat_ready, s + 1)
                nc.scalar.activation(rt_root[:, s, :], STAT[:, 0:TT], ACT.Sqrt, bias=eps[:, :], scale=1.0 / D).then_inc(root_ready, 1)

            loaded = [0]

            def preload(func):
                nc.scalar.activation(small[:, 33 + loaded[0]:34 + loaded[0]], eps[:, :], func)
                loaded[0] += 1

            def split_high(e, k):
                act.wait_ge(x_ready, KD * e + k + 1)
                if e < 3:
                    if not k and e:
                        act.wait_ge(unit_used, (FFN1 + N_UP + N_DOWN, OUT + KD)[e - 1])
                    nc.scalar.activation(XH[:, k, :], xT[:, k, :], ACT.Copy, scale=gains[:, 2 * e, k:k + 1]).then_inc(xh_ready, 1)
                    if k >= 2:
                        act.wait_ge(x_summed, KD * e + k - 1)
                    nc.scalar.activation(SQX[:, k % 2, :], xT[:, k, :], ACT.Square).then_inc(x_squared, 1)

            def square_y(m, count, buf):
                act.wait_ge(y_copied, count + m + 3)
                if m >= 2 or count:
                    act.wait_ge(y_summed, count + m - 1)
                nc.scalar.activation(SQ[:, m % 2, :], buf[:, m, :], ACT.Square).then_inc(y_squared, 1)

            def ffn(f, first):
                for k in range(KD):
                    split_high(2 * f, k)
                if not f:
                    act.wait_ge(lb_max, 1)
                    nc.scalar.activation(lbr, lbr, ACT.Exp).then_inc(lb_exp, 1)
                    preload(ACT.Sqrt)
                root(4 * f)
                preload(ACT.Sigmoid)

                def sig(j, a):
                    act.wait_ge(gate_scaled, j)
                    nc.scalar.activation(SQX[:, a, :], TMP[:, a, :], ACT.Sigmoid).then_inc(gate_sig, 1)

                with act.Fori(0, KF // 2 - 1) as i:
                    for a in range(2):
                        for b in range(2):
                            hi(first + NSLOT + 2 * a + b, i)
                        sig(i * 2 + (KF * f + a + 1), a)
                done[0] = first + N_UP
                for a in range(2):
                    ahead(first + N_UP + 2 * a + 1)
                    sig(KF * f + KF - 2 + a + 1, a)
                preload(ACT.Sqrt)
                for m in range(KD):
                    ahead(first + N_UP + 3 * m + 6)
                    square_y(m, 16 * f, YB)

            row = 0
            for name in ("ffn1_pre_norm", "ffn1_post_norm", "mix_pre_norm", "mix_post_norm", "ffn2_pre_norm", "ffn2_post_norm"):
                act.dma_start(vec_rows[row:row + KD, :], io[name][0].rearrange("(k p) -> k p", p=P)).then_inc(const_in, 16)
                row += KD
            for name in ("hgrn_lb_fwd", "hgrn_lb_bwd"):
                act.dma_start(vec_rows[row:row + 2 * NH, :], io[name].rearrange("r (h p) -> (r h) p", p=P)).then_inc(const_in, 16)
                row += 2 * NH
            act.dma_start(vec_rows[row:row + 4, :], io["attn_out_norm"][0].rearrange("(k p) -> k p", p=P)).then_inc(const_in, 16)
            act.dma_start(sink[:, :], io["attn_sink"][0].partition_broadcast(P)).then_inc(const_in, 16)
            act.dma_start(HGN[:, :], io["hgrn_out_norm"][0].partition_broadcast(P)).then_inc(const_in, 16)
            ahead(3)
            act.wait_ge(set_up, 1)
            ffn(0, FFN1)
            root(1)
            for k in range(KD):
                split_high(1, k)
            root(2)
            preload(ACT.Sigmoid)

            nsig = [0]

            def wide_sigmoid(used, before):
                act.wait_ge(unit_used, used)
                for c in range(TT):
                    if c >= 2:
                        act.wait_ge(proj_taken, before + c - 1)
                    nc.scalar.activation(SQX[:, c % 2, :], ps[c][:, :], ACT.Sigmoid, scale=rt[:, 2, c:c + 1]).then_inc(wide_sig, 1)

            def head_sigmoid(n):
                h, t = MIXU[n][1:]
                act.wait_ge(proj_taken, taken(n))
                nc.scalar.activation(Qh[:, h % 2, :] if t == 0 else Fg[:, h % 2, t - 1, :], TMP[:, NARROW.index(n) % 2, :],
                                     ACT.Sigmoid).then_inc(proj_sig, 1)

            ahead(MIX + 3)
            for n in range(3):
                ahead(MIX + n + 3)
                head_sigmoid(n)
            ahead(MIX + 3 + 4 + 2)
            wide_sigmoid(MIX + 3 + 4, 3)
            at = 3 + 4
            for what, n, g in (x + (0,) if len(x) == 2 else x for x in SCHEDULE):
                ahead(MIX + at + 3)
                if what == "half" and g:
                    at = n + 1
                    if MIXU[n][0] == "head":
                        head_sigmoid(n)
                elif what == "score" and g >= 8:
                    act.wait_ge(scores_ready, 11 * n + 1 + g)
                    if n:
                        act.wait_ge(pv_done, n)
                    nc.scalar.activation(SX[:, g - 8, :], ps[4 + (11 * n + g) % 2][:, :], ACT.Copy).then_inc(scores_copied, 1)
                elif what == "values":
                    act.wait_ge(pv_done, n + 1)
                    nc.scalar.activation(OS[:, :, n * P:(n + 1) * P], BC[:, :].rearrange("p (c v) -> p c v", c=TT), ACT.Copy)\
                        .then_inc(o_copied, 1)
            for c in range(TT):
                act.wait_ge(o_copied, NH)
                if c >= 2:
                    act.wait_ge(osq, c - 1)
                nc.scalar.activation(SQ[:, c % 2, :], OS[:, c, :], ACT.Square).then_inc(achain, 1)
            act.wait_ge(osq, TT)
            nc.scalar.activation(oroot, oss, ACT.Sqrt, bias=eps[:, :], scale=1.0 / P).then_inc(oroot_ready, 1)
            preload(ACT.Exp)
            ahead(OUT + 2)

            def split_mix(i):
                t = MIX_ORDER[i]
                if t >= 4:
                    act.wait_ge(mix_turned, i + 1)
                    nc.scalar.activation(XH[:, t, :], ps[6][:, :], ACT.Copy).then_inc(mixh, 1)
                else:
                    act.wait_ge(att_tmp, t + 1)
                    nc.scalar.activation(XH[:, t, :], TMP[:, t % 2, :], ACT.Copy, scale=attgain[:, t:t + 1]).then_inc(mixh, 1)

            for b in range(TT + 1):
                if b < TT:
                    act.wait_ge(nm_ready, b + 1)
                for n in range(HQ):
                    if b > 1 and n == 3:
                        split_mix(b - 2)
                    if b < TT:
                        nk = 3 if 0 < b < TT - 1 else 2
                        w = S[:, b % 2, n, 0:nk * P]
                        nc.scalar.activation(w, w, ACT.Exp, bias=nm8[b % 2][:, n:n + 1], scale=SCALE,
                                             accum_out=l8[b % 2][:, n:n + 1]).then_inc(s_exp, 1)
                        if n == HQ - 1:
                            nc.scalar.activation(e8[b % 2], e8[b % 2], ACT.Exp).then_inc(s_soft, 1)
                    if b and n % 2:
                        c = b - 1
                        nk = 3 if 0 < c < TT - 1 else 2
                        act.wait_ge(pt_ready, HQ * c + n + 1)
                        if HQ * c + n >= 2:
                            act.wait_ge(att_pv_done, HQ * c + n - 1)
                        nc.scalar.activation(PT[:, 1, 0:nk * P], ps[1][:, 0:nk * P], ACT.Copy).then_inc(pt_odd, 1)
                if b == 0:
                    wide_sigmoid(OUT, ALL_TAKEN)
                    preload(ACT.Exp)
                    ahead(OUT + 3)
                if b == TT:
                    preload(ACT.Sqrt)
                if b:
                    act.wait_ge(att_copied, b)
                    if b > 2:
                        act.wait_ge(att_sum, b - 2)
                    nc.scalar.activation(SQ[:, (b - 1) % 2, :].rearrange("p (f q) -> p f q", f=TT),
                                         ATT[:, :, (b - 1) * P:b * P], ACT.Square).then_inc(att_sq, 1)
            split_mix(TT - 1)
            act.wait_ge(att_stat, 1)
            nc.scalar.activation(aroot, STAT[:, TT:2 * TT], ACT.Sqrt, bias=eps[:, :], scale=1.0 / (HQ * DH)).then_inc(aroot_ready, 1)
            for i in range(4, KD):
                split_mix(i)
            for m in range(KD):
                ahead(OUT + m + 4)
                square_y(m, 8, YM)
            root(3)
            ffn(1, FFN2)
            root(5)
            for half, c in ((0, 0), (0, 1), (0, 2), (0, 3), (1, 1), (1, 3)):
                act.wait_ge(out_turned, half + 1)
                nc.scalar.activation(xout[:, c, half * 512:(half + 1) * 512], BACK[half][c][:, :], ACT.Copy).then_inc(out_copied, 1)

        @block.tensor
        def _(pe):
            def three(dst, s, k, xh, xl, first, last):
                w = slice(k * P, (k + 1) * P)
                nc.tensor.matmul(dst, WH[:, s, w], xh, start=first, stop=False)
                nc.tensor.matmul(dst, WH[:, s, w], xl, start=False, stop=False)
                return nc.tensor.matmul(dst, WL[:, s, w], xh, start=False, stop=last)

            def abreast(first, banks, e):
                for k in range(KD):
                    pe.wait_ge(xl_ready, KD * e + k + 1)
                    pe.wait_ge(xh_ready, KD * e + k + 1)
                    if k == KD - (1 if e else 2):
                        stat(2 * e, SSX, x_summed, KD * e + KD)
                    if k == KD - 1 and not e:
                        spread(0)
                    for u, bank in enumerate(banks):
                        if not k and first + u < 2:
                            pe.wait_ge(lo_first, first + u + 1)
                        elif not k:
                            pe.wait_ge(lo_done, first + u + 1)
                        mm = three(bank[:, :], (first + u) % NSLOT, k, XH[:, k, :], XL[:, k, :], not k, k == KD - 1)
                        if k == KD - 1:
                            mm.then_inc(unit_used, 1)
                if e:
                    spread(2 * e)

            def stat(s, sums, ready, count):
                pe.wait_ge(ready, count)
                for c in range(TT):
                    mm = nc.tensor.matmul(STAT[:, c:c + 1], sums[:, c * P:(c + 1) * P], ones[:, :], start=True, stop=True)
                mm.then_inc(stat_ready, 1)

            def spread(s):
                pe.wait_ge(rt_ready, s + 1)
                for c in range(TT):
                    mm = nc.tensor.matmul(BC[:, c * P:(c + 1) * P], rt[:, s, c:c + 1].broadcast_to([P, P]), ident[:, :],
                                          start=True, stop=True)
                mm.then_inc(bc_ready, 1)

            def half(n, bank, p):
                if not p:
                    pe.wait_ge(lo_done, n + 1)
                for k in range(KD // 2 * p, KD // 2 * (p + 1)):
                    mm = three(bank[:, :], n % NSLOT, k, XH[:, k, :], XL[:, k, :], not k, k == KD - 1)
                if p:
                    mm.then_inc(unit_used, 1)

            def whole(n, quarter, bank, xh, xl, k0=0, nk=KD, first=True, last=True):
                pe.wait_ge(lo_done, quarter * NSLOT + (n + 1))
                for k in range(nk):
                    mm = three(bank[:, :], n % NSLOT, k, xh[:, k0 + k, :], xl[:, k0 + k, :],
                               first and not k, last and k == nk - 1)
                mm.then_inc(unit_used, 1)

            def ffn(f, first):
                abreast(first, ps[0:4], 2 * f)
                with pe.Fori(0, KF // 2 - 1) as i:
                    for a in range(2):
                        pe.wait_ge(up_scaled, i * 2 + (KF * f + a + 1))
                        for b in range(2):
                            whole(first + NSLOT + 2 * a + b, i, ps[2 * a + b], XH, XL)
                hh, hl = hid[f]
                with pe.Fori(0, 2) as i:
                    for m in range(4):
                        for u, (k0, nk) in enumerate(KSPLIT):
                            if m == 0:
                                pe.wait_ge(h_ready, KF * f + min(k0 + nk, KF))
                            if not u:
                                pe.wait_ge(y_copied, i * 4 + (16 * f + m + 1))
                            whole(first + N_UP + 3 * m + u, i * 3, ps[4 + m % 2], hh, hl, k0, nk, not u, u == 2)
                stat(4 * f + 1, SS, y_summed, 16 * f + KD)
                spread(4 * f + 1)

            pe.wait_ge(ident_in, 16)
            for k in range(KD):
                if k == 3:
                    pe.wait_ge(const_in, CONST_IN)
                    nc.tensor.transpose(ps[6][:, 0:NV], vec_rows[:, :], ident[0:NV, 0:NV]).then_inc(vecs_turned, 1)
                if k >= 3:
                    pe.wait_ge(x_ready, k - 2)
                for c in range(TT):
                    if not k:
                        pe.wait_ge(x_in[c], 16)
                    mm = nc.tensor.transpose(turn[k % 3][:, c * P:(c + 1) * P], xin[:, c, k * P:(k + 1) * P], ident[:, :])
                mm.then_inc(x_turned, 1)
            ffn(0, FFN1)

            def wide(n, k0, cs):
                s = n % NSLOT
                for c in cs:
                    for kk in range(2):
                        k, w, t = k0 + kk, slice(kk * 512, (kk + 1) * 512), slice(c * P, (c + 1) * P)
                        nc.tensor.matmul(ps[c][:, :], XH[:, k, t], WH[:, s, w], start=not k, stop=False)
                        nc.tensor.matmul(ps[c][:, :], XL[:, k, t], WH[:, s, w], start=False, stop=False)
                        mm = nc.tensor.matmul(ps[c][:, :], XH[:, k, t], WL[:, s, w], start=False, stop=k == KD - 1)
                if TT - 1 in cs:
                    mm.then_inc(unit_used, 1)

            def level_side(h, lv, side):
                half = 1 << lv
                q = W[:, h % 2, 0 if side else 3, :]
                return q.rearrange("p (c b s j) -> p c b s j", c=TT, s=2, j=half)[:, :, :, side, :]

            def scores(h, g):
                b, n = h % 2, 11 * h + g
                if n >= 2:
                    hp, gp = (n - 2) // 11, (n - 2) % 11
                    if gp < 8:
                        pe.wait_ge(scores_masked, 8 * hp + gp + 1)
                    else:
                        pe.wait_ge(scores_copied, 3 * hp + gp - 7)
                to = ps[4 + n % 2]
                if g < 2:
                    pe.wait_ge(base_ready, h + 1)
                else:
                    pe.wait_ge(tree_ready, 8 * h + min(g - 1, 8))
                if g == 0:
                    for c in range(TT):
                        t = slice(c * P, (c + 1) * P)
                        mm = nc.tensor.matmul(to[:, t], KS[:, b, t], Qh[:, b, t], start=True, stop=True)
                elif g < 8:
                    for side in range(2):
                        q = level_side(h, g - 1, side)
                        for c in range(TT):
                            mm = nc.tensor.matmul(to[:, side * 256 + c * 64:side * 256 + (c + 1) * 64],
                                                  W[:, b, 2 if side else 1, c * P:(c + 1) * P], q[:, c], start=True, stop=True)
                elif g == 8:
                    for c in range(TT):
                        o = c ^ 1
                        fwd = o > c
                        mm = nc.tensor.matmul(to[:, c * P:(c + 1) * P], W[:, b, 2 if fwd else 1, c * P:(c + 1) * P],
                                              W[:, b, 0 if fwd else 3, o * P:(o + 1) * P], start=True, stop=True)
                else:
                    back = g - 9
                    o = 256 * (1 - back)
                    for c in range(2):
                        ck = 2 * back + c
                        mm = nc.tensor.matmul(to[:, c * 256:(c + 1) * 256], W[:, b, 1 if back else 2, ck * P:(ck + 1) * P],
                                              W[:, b, 3 if back else 0, o:o + 256], start=True, stop=True)
                mm.then_inc(scores_ready, 1)

            def values(h):
                pe.wait_ge(scores_masked, 8 * h + 8)
                pe.wait_ge(scores_copied, 3 * h + 3)
                pe.wait_ge(proj_taken, 3 + TT)
                if h:
                    pe.wait_ge(o_copied, h)
                    if h > 1:
                        pe.wait_ge(va_ready, 1)
                else:
                    pe.wait_ge(rsb_ready, 2)
                for t in range(TT):
                    for n, c in enumerate(range(TT)):
                        if c == t:
                            s = SD[:, t * P:(t + 1) * P]
                        elif c == t ^ 1:
                            s = SX[:, 0, c * P:(c + 1) * P]
                        else:
                            at = (c % 2) * 256 + (t % 2) * P
                            s = SX[:, 1 + c // 2, at:at + P]
                        mm = nc.tensor.matmul(BC[:, t * P:(t + 1) * P], s, V[:, c, h * P:(h + 1) * P],
                                              start=not n, stop=n == TT - 1)
                mm.then_inc(pv_done, 1)

            def turn_unit(n):
                pe.wait_ge(proj_taken, taken(n))
                tmp = TMP[:, NARROW.index(n) % 2, :]
                if MIXU[n][0] == "v":
                    pe.wait_ge(o_copied, 1)
                    for c in range(TT):
                        mm = nc.tensor.transpose(BC[:, c * P:(c + 1) * P], tmp[:, c * P:(c + 1) * P], ident[:, :])
                    mm.then_inc(va_turned, 1)
                else:
                    r = TURNED.index(n)
                    pe.wait_ge(mix_in, MIX_IN)
                    if r:
                        pe.wait_ge(rope_done, r)
                    nc.tensor.matmul(ps[6][:, :], swap[:, :], tmp, start=True, stop=True).then_inc(rot_ready, 1)

            abreast(MIX, ps[0:3], 1)
            pe.wait_ge(proj_taken, 3)
            for u in range(4):
                pe.wait_ge(lo_done, MIX + 3 + u + 1)
                wide(MIX + 3 + u, 2 * u, range(TT))
            def att_scores(b):
                k0 = max(b - 1, 0)
                nk = 3 if 0 < b < TT - 1 else 2
                for n in range(HQ):
                    j, kv = n // 2, n % 2
                    r = slice(kv * DH, (kv + 1) * DH)
                    if HQ * b + n >= 2:
                        pe.wait_ge(s_max, HQ * b + n - 1)
                    nc.tensor.matmul(ps[4 + n % 2][:, 0:nk * P], qT[r, j, b * P:(b + 1) * P], kT[r, k0 * P:(k0 + nk) * P],
                                     start=True, stop=True).then_inc(s_ready, 1)

            for at, (what, n, g) in enumerate(x + (0,) if len(x) == 2 else x for x in SCHEDULE):
                if at == len(SCHEDULE) - 1:
                    pe.wait_ge(rope_done, len(TURNED))
                    pe.wait_ge(scores_copied, 3 * NH)
                    att_scores(0)
                if what == "score":
                    scores(n, g)
                elif what == "values":
                    values(n)
                elif what == "turn":
                    turn_unit(n)
                elif MIXU[n][0] == "hg":
                    if not g:
                        pe.wait_ge(proj_taken, ALL_TAKEN)
                        pe.wait_ge(lo_done, MIX + n + 1)
                    wide(MIX + n, MIXU[n][1], (0, 1) if not g else (2, 3))
                else:
                    if not g:
                        pe.wait_ge(proj_taken, bank_free(n))
                    half(MIX + n, ps[bank_of(n)], g)

            def att_values(b, n, k0, nk):
                pe.wait_ge((pt_even, pt_odd)[n % 2], 4 * b + n // 2 + 1)
                j, kv = n // 2, n % 2
                if not n:
                    pe.wait_ge(va_ready, 1)
                    if b:
                        pe.wait_ge(att_copied, b)
                head = kv * G + j
                to = BC[(head % 2) * DH:(head % 2 + 1) * DH, (head // 2) * P:(head // 2 + 1) * P]
                for c in range(nk):
                    mm = nc.tensor.matmul(to, VA[:, k0 + c, kv * DH:(kv + 1) * DH], PT[:, n % 2, c * P:(c + 1) * P],
                                          start=not c, stop=c == nk - 1)
                mm.then_inc(att_pv_done, 1)

            def att_turn(b):
                k0 = max(b - 1, 0)
                nk = 3 if 0 < b < TT - 1 else 2
                for n in range(HQ):
                    pe.wait_ge(s_norm, HQ * b + n + 1)
                    if 4 * b + n // 2:
                        pe.wait_ge((pt_even, pt_odd)[n % 2], 4 * b + n // 2)
                    else:
                        pe.wait_ge(proj_taken, ALL_TAKEN + TT)
                    for c in range(nk):
                        mm = nc.tensor.transpose(ps[n % 2][:, c * P:(c + 1) * P], S[:, b % 2, n, c * P:(c + 1) * P], ident[:, :])
                    mm.then_inc(pt_ready, 1)
                    if n:
                        att_values(b, n - 1, k0, nk)
                att_values(b, HQ - 1, k0, nk)

            def mix_turn(i):
                if i:
                    pe.wait_ge(mixl, i)
                else:
                    pe.wait_ge(hg_final, TT)
                f = slice(i * P, (i + 1) * P)
                for c in range(TT):
                    mm = nc.tensor.transpose(ps[6][:, c * P:(c + 1) * P], OS[:, c, f], ident[:, :])
                mm.then_inc(mix_turned, 1)

            def out_products(i, ms):
                t = MIX_ORDER[i]
                pe.wait_ge(mixl, i + 1)
                for m in ms:
                    if not i:
                        pe.wait_ge(lo_done, OUT + m + 1)
                    mm = three(OUT_BANK[m][:, :], (OUT + m) % NSLOT, t, XH[:, t, :], XL[:, t, :], not i, i == KD - 1)
                    if i == KD - 1:
                        mm.then_inc(unit_used, 1)

            for b in range(TT):
                if b + 1 < TT:
                    att_scores(b + 1)
                if b:
                    mix_turn(b - 1)
                if b > 1:
                    out_products(b - 2, (0, 1))
                att_turn(b)
            mix_turn(TT - 1)
            for i in (TT - 2, TT - 1):
                out_products(i, (0, 1))
            pe.wait_ge(s_max, HQ * TT)
            for i in range(TT):
                out_products(i, (2, 3))
                if i == 2:
                    pe.wait_ge(att_sum, TT)
                    for c in range(TT):
                        mm = nc.tensor.matmul(STAT[:, TT + c:TT + c + 1], SS[:, c * P:(c + 1) * P], ones[:, :], start=True, stop=True)
                    mm.then_inc(att_stat, 1)
            pe.wait_ge(arr_ready, 1)
            for c in range(TT):
                mm = nc.tensor.matmul(BC[:, c * P:(c + 1) * P], arr[:, c:c + 1].broadcast_to([P, P]), ident[:, :],
                                      start=True, stop=True)
            mm.then_inc(att_bc, 1)
            for i in range(TT, KD):
                out_products(i, range(4))
            for m in range(4, KD):
                if m >= 6:
                    pe.wait_ge(y_copied, KD + m + 1)
                else:
                    pe.wait_ge(mixl, KD)
                whole(OUT + m, 0, OUT_BANK[m], XH, XL)
            stat(3, SS, y_summed, 2 * KD)
            spread(3)
            ffn(1, FFN2)
            for k in range(KD):
                pe.wait_ge(x_ready, 3 * KD + k + 1)
                for c in range(TT):
                    if k == KD // 2 and c == TT - 1:
                        pe.wait_ge(out_copied, 1)
                    bank = BACK[k // 4][c]
                    mm = nc.tensor.transpose(bank[:, k % 4 * P:(k % 4 + 1) * P], xT[:, k, c * P:(c + 1) * P], ident[:, :])
                if k % 4 == 3:
                    mm.then_inc(out_turned, 1)

        @block.vector
        def _(dve):
            steps = [0]

            def step(ins):
                ins.then_inc(vchain, 1)
                steps[0] += 1
                dve.wait_ge(vchain, steps[0])

            def split_low(e, k):
                dve.wait_ge(xh_ready, KD * e + k + 1)
                nc.vector.scalar_tensor_tensor(out=XL[:, k, :], in0=xT[:, k, :], scalar=gains[:, 2 * e, k:k + 1],
                                               in1=XH[:, k, :].bitcast(fp32), op0=ALU.mult, op1=ALU.subtract).then_inc(xl_ready, 1)

            def inverse(s):
                dve.wait_ge(root_ready, s + 1)
                nc.vector.reciprocal(rt[:, s, :], rt_root[:, s, :]).then_inc(rt_ready, 1)

            def take_rms(e):
                inverse(2 * e)
                dve.wait_ge(bc_ready, 2 * e + 1)
                nc.vector.tensor_copy(RSB[:, :], BC[:, :]).then_inc(rsb_ready, 1)
                dve.wait_ge(rsb_ready, e + 1)

            def add_norm(e, buf):
                s = 2 * e - 1
                inverse(s)
                dve.wait_ge(bc_ready, s + 1)
                for k in range(KD):
                    step(nc.vector.tensor_tensor(TMP[:, k % 2, :], buf[:, k, :], BC[:, :], ALU.mult))
                    nc.vector.scalar_tensor_tensor(out=xT[:, k, :], in0=TMP[:, k % 2, :], scalar=gains[:, s, k:k + 1],
                                                   in1=xT[:, k, :], op0=ALU.mult, op1=ALU.add).then_inc(x_ready, 1)
                    if k and e < 3:
                        split_low(e, k - 1)
                if e < 3:
                    split_low(e, KD - 1)

            def clear_sum():
                step(nc.vector.memset(SS[:, :], 0.0))

            def take_y(m, used, count, buf, bank=None):
                dve.wait_ge(unit_used, used)
                bank = bank or ps[4 + m % 2]
                nc.vector.tensor_copy(buf[:, m, :], bank[:, :]).then_inc(y_copied, 1)
                if m:
                    add_square(m - 1, count)
                if m == KD - 1:
                    add_square(m, count)

            def add_square(m, count):
                dve.wait_ge(y_squared, count + m + 1)
                if m:
                    dve.wait_ge(y_summed, count + m)
                nc.vector.tensor_tensor(SS[:, :], SS[:, :], SQ[:, m % 2, :], ALU.add).then_inc(y_summed, 1)

            def ffn(f, first):
                hh, hl = hid[f]
                take_rms(2 * f)
                clear_sum()
                base = steps[0]
                with dve.Fori(0, KF // 2) as i:
                    for a in range(2):
                        n = i * 2 + (KF * f + a + 1)
                        dve.wait_ge(unit_used, i * NSLOT + (first + 2 * a + 1))
                        nc.vector.tensor_tensor(TMP[:, a, :], ps[2 * a][:, :], RSB[:, :], ALU.mult).then_inc(gate_scaled, 1)
                        dve.wait_ge(unit_used, i * NSLOT + (first + 2 * a + 2))
                        nc.vector.tensor_tensor(SQ[:, a, :], ps[2 * a + 1][:, :], RSB[:, :], ALU.mult).then_inc(up_scaled, 1)
                        dve.wait_ge(up_scaled, n)
                        nc.vector.tensor_tensor(SQ[:, a, :], SQ[:, a, :], TMP[:, a, :], ALU.mult).then_inc(vchain, 1)
                        dve.wait_ge(vchain, i * 6 + (base + 3 * a + 1))
                        dve.wait_ge(gate_sig, n)
                        nc.vector.tensor_tensor(SQ[:, a, :], SQ[:, a, :], SQX[:, a, :], ALU.mult).then_inc(vchain, 1)
                        dve.wait_ge(vchain, i * 6 + (base + 3 * a + 2))
                        j = i * 2 + a
                        nc.vector.tensor_copy(hh[:, j, :], SQ[:, a, :]).then_inc(vchain, 1)
                        dve.wait_ge(vchain, i * 6 + (base + 3 * a + 3))
                        nc.vector.tensor_tensor(hl[:, j, :], SQ[:, a, :], hh[:, j, :].bitcast(fp32), ALU.subtract).then_inc(h_ready, 1)
                steps[0] += 3 * KF
                for m in range(KD):
                    take_y(m, first + N_UP + len(KSPLIT) * (m + 1), 16 * f, YB)

            nc.vector.memset(ones[:, :], 1.0).then_inc(y_copied, 1)
            nc.vector.memset(eps[:, :], EPS).then_inc(y_copied, 1)
            def take_x(k):
                dve.wait_ge(x_turned, k + 1)
                nc.vector.tensor_copy(xT[:, k, :], turn[k % 3][:, :]).then_inc(x_ready, 1)

            for k in range(3):
                take_x(k)
            for u in range(2):
                dve.wait_ge(hi_done, u + 1)
                nc.vector.tensor_tensor(WL[:, u, :], raw[:, u, :], WH[:, u, :].bitcast(fp32), ALU.subtract).then_inc(lo_first, 1)
            dve.wait_ge(vecs_turned, 1)
            step(nc.vector.tensor_copy(vecs[:, :], ps[6][:, 0:NV]))
            nc.vector.tensor_scalar(gains[:, 1, :], gains[:, 1, :], 0.5, None, ALU.mult)
            step(nc.vector.tensor_scalar(gains[:, 5, :], gains[:, 5, :], 0.5, None, ALU.mult))
            step(nc.vector.tensor_tensor(lbm.rearrange("p (d h) -> p d h", d=2), lbr[:, :, 0, :], lbr[:, :, 1, :], ALU.max))
            nc.vector.tensor_tensor(lbr[:, :, 0, :], lbr[:, :, 0, :], lbm.rearrange("p (d h) -> p d h", d=2), ALU.subtract)
            nc.vector.tensor_tensor(lbr[:, :, 1, :], lbr[:, :, 1, :], lbm.rearrange("p (d h) -> p d h", d=2),
                                    ALU.subtract).then_inc(lb_max, 1)
            dve.wait_ge(const_in, CONST_IN)
            nc.vector.memset(small[:, 32:33], 0.0).then_inc(set_up, 1)
            for k in range(KD):
                if k >= 3:
                    take_x(k)
                if k:
                    split_low(0, k - 1)
            split_low(0, KD - 1)
            dve.wait_ge(lb_exp, 1)
            step(nc.vector.tensor_tensor(lbs.rearrange("p (d h) -> p d h", d=2), lbr[:, :, 0, :], lbr[:, :, 1, :], ALU.add))
            step(nc.vector.reciprocal(lbs, lbs))
            step(nc.vector.tensor_tensor(lb.rearrange("p (d h) -> p d h", d=2), lbr[:, :, 0, :],
                                         lbs.rearrange("p (d h) -> p d h", d=2), ALU.mult))
            step(nc.vector.tensor_scalar(lb1, lb, -1.0, 1.0, ALU.mult, ALU.add))
            ffn(0, FFN1)
            add_norm(1, YB)

            take_rms(1)

            def scale_unit(n):
                i = NARROW.index(n)
                dve.wait_ge(unit_used, MIX + n + 1)
                if i >= 2:
                    last = NARROW[i - 2]
                    if MIXU[last][0] == "head":
                        dve.wait_ge(proj_sig, HEADED.index(last) + 1)
                    elif MIXU[last][0] == "v":
                        dve.wait_ge(va_turned, 1)
                    else:
                        dve.wait_ge(rot_ready, TURNED.index(last) + 1)
                nc.vector.tensor_tensor(TMP[:, i % 2, :], ps[bank_of(n)][:, :], RSB[:, :], ALU.mult).then_inc(proj_taken, 1)

            def gates(h):
                b = h % 2
                dve.wait_ge(proj_sig, 3 * h + 3)
                for d in range(2):
                    at = 4 * d + h
                    step(nc.vector.tensor_scalar(Fg[:, b, d, :], Fg[:, b, d, :], lb1[:, at:at + 1], lb[:, at:at + 1], ALU.mult, ALU.add))
                if h >= 2:
                    dve.wait_ge(pv_done, h - 1)
                nc.vector.tensor_scalar(W[:, b, 2, :], Fg[:, b, 0, :], -1.0, 1.0, ALU.mult, ALU.add)
                step(nc.vector.tensor_scalar(W[:, b, 1, :], Fg[:, b, 1, :], -1.0, 1.0, ALU.mult, ALU.add))
                nc.vector.tensor_tensor(W[:, b, 0, :], Qh[:, b, :], Fg[:, b, 0, :], ALU.mult)
                nc.vector.tensor_tensor(W[:, b, 3, :], Qh[:, b, :], Fg[:, b, 1, :], ALU.mult)
                nc.vector.tensor_tensor(KS[:, b, :], W[:, b, 1, :], W[:, b, 2, :], ALU.add).then_inc(base_ready, 1)

            GOFF = [0, 0, 256, 384, 448, 480, 496, 504, 508]

            def whole_decay(h, lv):
                if lv == 0:
                    return Fg[:, h % 2, :, :]
                return GT[:, :, GOFF[lv]:GOFF[lv] + (TOK >> lv)]

            def grow(h, lv):
                b, half = h % 2, 1 << lv
                if lv:
                    dve.wait_ge(tree_ready, 8 * h + lv)
                else:
                    dve.wait_ge(base_ready, h + 1)
                g = whole_decay(h, lv).rearrange("p d (b s) -> p d b s", s=2)
                if lv < 7:
                    nc.vector.tensor_tensor(whole_decay(h, lv + 1), g[:, :, :, 0], g[:, :, :, 1], ALU.mult)
                dve.wait_ge(scores_ready, 11 * h + 2 + lv)
                for side in range(2):
                    w = W[:, b, (2, 0)[side]:(4, 2)[side], :].rearrange("p a (b s j) -> p a b s j", s=2, j=half)[:, :, :, side, :]
                    if half == 1:
                        w = w.rearrange("p a b j -> p a (b j)")
                        by = g[:, :, :, 1 - side]
                    else:
                        by = g[:, :, :, 1 - side].unsqueeze(3).broadcast_to([P, 2, TOK // (2 * half), half])
                    ins = nc.vector.tensor_tensor(w, w, by, ALU.mult)
                ins.then_inc(tree_ready, 1)

            def diagonal(h):
                dve.wait_ge(scores_ready, 11 * h + 1)
                if h:
                    dve.wait_ge(pv_done, h)
                nc.vector.tensor_tensor(SD[:, :].rearrange("p (c t) -> p c t", c=TT),
                                        ps[4 + 11 * h % 2][:, :].rearrange("p (c t) -> p c t", c=TT),
                                        ident[:, :].unsqueeze(1).broadcast_to([P, TT, P]), ALU.mult).then_inc(scores_masked, 1)

            def take_level(h, lv):
                half = 1 << lv
                dve.wait_ge(scores_masked, 8 * h + 1 + lv)
                nc.vector.copy_predicated(SD[:, :].rearrange("p (b s j) -> p s b j", s=2, j=half), masks[:, lv, :],
                                          ps[4 + (11 * h + 1 + lv) % 2][:, :]).then_inc(scores_masked, 1)

            def values_in(used, to, gain, cs=range(TT)):
                dve.wait_ge(unit_used, used)
                for c in cs:
                    dve.wait_ge(wide_sig, (TT if gain else 0) + c + 1)
                    nc.vector.scalar_tensor_tensor(out=to[:, c, :], in0=ps[c][:, :], scalar=rt[:, 2, c:c + 1],
                                                   in1=SQX[:, c % 2, :], op0=ALU.mult, op1=ALU.mult).then_inc(proj_taken, 1)

            def turned(n):
                if MIXU[n][0] == "v":
                    dve.wait_ge(va_turned, 1)
                    nc.vector.tensor_copy(VA[:, :, :], BC[:, :].rearrange("p (c d) -> p c d", c=TT)).then_inc(va_ready, 1)
                    return
                dve.wait_ge(proj_taken, taken(n))
                to = kT[:, :] if MIXU[n][0] == "k" else qT[:, MIXU[n][1], :]
                step(nc.vector.tensor_tensor(SQ[:, 0, :], TMP[:, NARROW.index(n) % 2, :], rope[:, 0, :], ALU.mult))
                dve.wait_ge(rot_ready, TURNED.index(n) + 1)
                step(nc.vector.tensor_tensor(to, ps[6][:, :], rope[:, 1, :], ALU.mult))
                nc.vector.tensor_tensor(to, to, SQ[:, 0, :], ALU.add).then_inc(rope_done, 1)

            for n in range(3):
                scale_unit(n)
            gates(0)
            dve.wait_ge(mix_in, MIX_IN)
            step(nc.vector.tensor_copy(masks[:, :, :], mask_in[:, :, :]))
            values_in(MIX + 3 + 4, V, False)
            for what, n, g in (x + (0,) if len(x) == 2 else x for x in SCHEDULE):
                if what == "score":
                    if g == 0:
                        diagonal(n)
                    elif g < 8:
                        grow(n, g - 1)
                        take_level(n, g - 1)
                    elif g == 8:
                        grow(n, 7)
                elif what == "turn":
                    turned(n)
                elif what == "half" and g and n in NARROW:
                    scale_unit(n)
                    if MIXU[n][0] == "head" and MIXU[n][2] == 2:
                        gates(MIXU[n][1])

            def by_pair(x):
                return x.rearrange("p (j s) -> p j s", s=HKV)

            def att_max(b, n):
                nk = 3 if 0 < b < TT - 1 else 2
                at, e = 0 if b else P, b % 2
                if b >= 2:
                    dve.wait_ge(pt_ready, HQ * (b - 1))
                dve.wait_ge(s_ready, HQ * b + n + 1)
                nc.vector.tensor_tensor_reduce(out=S[:, e, n, 0:nk * P], in0=ps[4 + n % 2][:, 0:nk * P],
                                               in1=band[:, at:at + nk * P], scale=1.0, scalar=-3e38,
                                               op0=ALU.add, op1=ALU.max, accum_out=m8[e][:, n:n + 1]).then_inc(s_max, 1)

            def att_shift(b):
                e = b % 2
                dve.wait_ge(s_max, HQ * (b + 1))
                sk = sink[:, :].rearrange("p (s j) -> p j s", s=HKV)
                step(nc.vector.scalar_tensor_tensor(out=by_pair(m8[e]), in0=by_pair(m8[e]), scalar=SCALE, in1=sk, op0=ALU.mult, op1=ALU.max))
                nc.vector.tensor_scalar(nm8[e], m8[e], -1.0, None, ALU.mult)
                nc.vector.tensor_tensor(by_pair(e8[e]), sk, by_pair(m8[e]), ALU.subtract).then_inc(nm_ready, 1)

            def weights_sum(b):
                e = b % 2
                dve.wait_ge(s_soft, b + 1)
                step(nc.vector.tensor_tensor(r8[e], l8[e], e8[e], ALU.add))
                step(nc.vector.reciprocal(r8[e], r8[e]))

            def weights_norm(b, n):
                nk = 3 if 0 < b < TT - 1 else 2
                w = S[:, b % 2, n, 0:nk * P]
                nc.vector.tensor_scalar(w, w, r8[b % 2][:, n:n + 1], None, ALU.mult).then_inc(s_norm, 1)

            def split_mix_low(i):
                t = MIX_ORDER[i]
                dve.wait_ge(mixh, i + 1)
                if t >= 4:
                    ins = nc.vector.tensor_tensor(XL[:, t, :], ps[6][:, :], XH[:, t, :].bitcast(fp32), ALU.subtract)
                else:
                    ins = nc.vector.scalar_tensor_tensor(out=XL[:, t, :], in0=TMP[:, t % 2, :], scalar=attgain[:, t:t + 1],
                                                         in1=XH[:, t, :].bitcast(fp32), op0=ALU.mult, op1=ALU.subtract)
                ins.then_inc(mixl, 1)

            def att_take(b):
                nk = 3 if 0 < b < TT - 1 else 2
                for n in range(0, HQ, 2):
                    dve.wait_ge(pt_ready, HQ * b + n + 1)
                    if HQ * b + n >= 2:
                        dve.wait_ge(att_pv_done, HQ * b + n - 1)
                    nc.vector.tensor_copy(PT[:, 0, 0:nk * P], ps[0][:, 0:nk * P]).then_inc(pt_even, 1)
                    if b and n == 4:
                        split_mix_low(b - 1)
                dve.wait_ge(att_pv_done, HQ * (b + 1))
                nc.vector.tensor_copy(ATT[:, :, b * P:(b + 1) * P], BC[:, :].rearrange("p (f q) -> p f q", f=TT)).then_inc(att_copied, 1)

            def sum_att(b):
                dve.wait_ge(att_sq, b + 1)
                nc.vector.reduce_sum(SS[:, b * P:(b + 1) * P], SQ[:, b % 2, :].rearrange("p (f q) -> p q f", f=TT), AX.X).then_inc(att_sum, 1)

            dve.wait_ge(pv_done, NH)
            for n in range(HQ):
                att_max(0, n)
                if n >= TT:
                    c = n - TT
                    dve.wait_ge(achain, c + 1)
                    nc.vector.reduce_sum(oss[:, NH * c:NH * (c + 1)], SQ[:, c % 2, :].rearrange("p (h v) -> p h v", h=NH), AX.X).then_inc(osq, 1)
            att_shift(0)
            dve.wait_ge(oroot_ready, 1)
            nc.vector.reciprocal(orr, oroot).then_inc(orr_ready, 1)
            for b in range(TT):
                for n in range(HQ):
                    if b + 1 < TT:
                        att_max(b + 1, n)
                    if not b and n >= HQ - TT:
                        values_in(OUT, HGATE, True, (n - (HQ - TT),))
                    if n == 2:
                        weights_sum(b)
                    for head in ((), (), (), (0,), (1,), (2, 3), (4, 5), (6, 7))[n]:
                        weights_norm(b, head)
                if b + 1 < TT:
                    att_shift(b + 1)
                if b:
                    sum_att(b - 1)
                att_take(b)
            split_mix_low(TT - 1)
            sum_att(TT - 1)
            dve.wait_ge(aroot_ready, 1)
            nc.vector.reciprocal(arr, aroot).then_inc(arr_ready, 1)
            dve.wait_ge(att_bc, 1)
            for t in range(TT):
                if t >= 2:
                    dve.wait_ge(mixl, TT + t - 1)
                nc.vector.tensor_tensor(TMP[:, t % 2, :], ATT[:, t, :], BC[:, :], ALU.mult).then_inc(att_tmp, 1)
                if t:
                    split_mix_low(TT + t - 1)
            split_mix_low(KD - 1)
            clear_sum()
            for m in range(KD):
                take_y(m, OUT + m + 1, KD, YM, OUT_BANK[m])
            add_norm(2, YM)
            ffn(1, FFN2)
            add_norm(3, YB)
            dve.wait_ge(out_turned, 2)
            for c in (0, 2):
                nc.vector.tensor_copy(xout[:, c, 512:1024], BACK[1][c][:, :]).then_inc(out_copied_v, 1)


def kernel(**inputs):
    import concourse.bacc as bacc
    from concourse.bass_utils import run_bass_kernel_spmd

    nc = bacc.Bacc("TRN2", target_bir_lowering=False, num_devices=1)
    arrays = {name: np.ascontiguousarray(a) for name, a in inputs.items()}
    arrays.update(host_tables())
    io = {name: nc.dram_tensor(name, a.shape, mybir.dt.from_np(a.dtype), kind="ExternalInput").ap() for name, a in arrays.items()}
    out = nc.dram_tensor("out", (1, TOK, D), mybir.dt.float32, kind="ExternalOutput").ap()
    encoder_layer(nc, io, out)
    r = run_bass_kernel_spmd(nc, [arrays], core_ids=[0])
    return r.results[0]["out"]
```
